# Optimizing a Trainium2 kernel written in Bass

```python
import jax, jax.numpy as jnp
from jax import lax
import numpy as np

D_MODEL = 1024
BATCH = 1
SEQ = 256
DEPTH = 2

CHUNK = 64
N_MIXERS = 2
N_ATTN_LAYERS = (DEPTH + 1) // 2
N_REC_LAYERS = DEPTH // 2

ATTN_HEADS = 16
HEAD_DIM = D_MODEL // ATTN_HEADS
LEFT_CHUNKS = 8
BAND = (LEFT_CHUNKS + 1) * CHUNK
REL_CLIP = 256
N_REL = 2 * REL_CLIP + 1
NEG_INF = -1e30

LRU_WIDTH = D_MODEL
LRU_HEADS = 4
LRU_BLOCK = LRU_WIDTH // LRU_HEADS
CONV_WIDTH = 4
LRU_C = 8.0

PEER_HEADS = 8
N_KEYS = 128
N_EXPERTS = N_KEYS * N_KEYS
PEER_TOPK = 16
D_KEY = 256
D_HALF = D_KEY // 2
PEER_TOKEN_BLOCK = 128

EPS = 1e-6

kernel_name = "hybrid_chunkattn_rglru_peer"

def rms_norm(x, g):
    xf = x.astype(jnp.float32)
    y = xf * lax.rsqrt(jnp.mean(xf * xf, axis=-1, keepdims=True) + EPS)
    return (y * g.astype(jnp.float32)).astype(x.dtype)

def rel_bias(table):
    i = jnp.arange(CHUNK)[:, None]
    j = jnp.arange(BAND)[None, :]
    dist = LEFT_CHUNKS * CHUNK + i - j
    idx = jnp.clip(dist, -REL_CLIP, REL_CLIP) + REL_CLIP
    return table[:, idx]

def chunk_attention(x, w_qkv, q_g, k_g, bias_table, w_out):
    b, s, _ = x.shape
    n_chunks = s // CHUNK
    q, k, v = jnp.split(x @ w_qkv, 3, axis=-1)
    q = rms_norm(q.reshape(b, s, ATTN_HEADS, HEAD_DIM), q_g)
    k = rms_norm(k.reshape(b, s, ATTN_HEADS, HEAD_DIM), k_g)
    v = v.reshape(b, s, ATTN_HEADS, HEAD_DIM)
    pad = ((0, 0), (LEFT_CHUNKS * CHUNK, 0), (0, 0), (0, 0))
    k_pad = jnp.pad(k, pad)
    v_pad = jnp.pad(v, pad)
    bias = rel_bias(bias_table).astype(jnp.float32)
    scale = HEAD_DIM ** -0.5
    key_off = jnp.arange(BAND)

    def one_chunk(c):
        start = c * CHUNK
        q_c = lax.dynamic_slice_in_dim(q, start, CHUNK, axis=1)
        k_c = lax.dynamic_slice_in_dim(k_pad, start, BAND, axis=1)
        v_c = lax.dynamic_slice_in_dim(v_pad, start, BAND, axis=1)
        scores = jnp.einsum('bqhd,bkhd->bhqk', q_c, k_c,
                            preferred_element_type=jnp.float32) * scale + bias
        valid = (key_off + start) >= LEFT_CHUNKS * CHUNK
        scores = jnp.where(valid, scores, NEG_INF)
        p = jax.nn.softmax(scores, axis=-1).astype(v.dtype)
        return jnp.einsum('bhqk,bkhd->bqhd', p, v_c)

    out = lax.map(one_chunk, jnp.arange(n_chunks))
    out = jnp.moveaxis(out, 0, 1).reshape(b, s, D_MODEL)
    return out @ w_out

def rglru_mixer(x, w_in, conv_w, conv_b, w_a, b_a, w_x, b_x, lam, w_out):
    b, s, _ = x.shape
    gate, u = jnp.split(x @ w_in, 2, axis=-1)
    u = lax.conv_general_dilated(
        u, conv_w[:, None, :], window_strides=(1,), padding=[(CONV_WIDTH - 1, 0)],
        dimension_numbers=('NWC', 'WIO', 'NWC'), feature_group_count=LRU_WIDTH) + conv_b
    uh = u.reshape(b, s, LRU_HEADS, LRU_BLOCK)
    r = jax.nn.sigmoid(jnp.einsum('bshi,hij->bshj', uh, w_a).reshape(b, s, LRU_WIDTH) + b_a)
    i = jax.nn.sigmoid(jnp.einsum('bshi,hij->bshj', uh, w_x).reshape(b, s, LRU_WIDTH) + b_x)
    log_a = -LRU_C * r.astype(jnp.float32) * jax.nn.softplus(-lam.astype(jnp.float32))
    a = jnp.exp(log_a)
    mult = jnp.sqrt(-jnp.expm1(2.0 * log_a))
    bx = mult * (i * u).astype(jnp.float32)

    def combine(left, right):
        a_l, b_l = left
        a_r, b_r = right
        return a_l * a_r, a_r * b_l + b_r

    _, h = lax.associative_scan(combine, (a, bx), axis=1)
    y = jax.nn.gelu(gate) * h.astype(x.dtype)
    return y @ w_out

def peer_ffn(h, w_q, sub_keys, u_tab, v_tab):
    b, s, d = h.shape
    t = b * s
    blocks = h.reshape(t // PEER_TOKEN_BLOCK, PEER_TOKEN_BLOCK, d)

    def one_block(xb):
        tb = xb.shape[0]
        q = (xb @ w_q).reshape(tb, PEER_HEADS, 2, D_HALF)
        s_half = jnp.einsum('thpc,pnc->thpn', q, sub_keys,
                            preferred_element_type=jnp.float32)
        top_s, top_i = lax.top_k(s_half, PEER_TOPK)
        cand = (top_s[:, :, 0, :, None] + top_s[:, :, 1, None, :]).reshape(
            tb, PEER_HEADS, PEER_TOPK * PEER_TOPK)
        best_s, best_c = lax.top_k(cand, PEER_TOPK)
        i1 = jnp.take_along_axis(top_i[:, :, 0], best_c // PEER_TOPK, axis=-1)
        i2 = jnp.take_along_axis(top_i[:, :, 1], best_c % PEER_TOPK, axis=-1)
        expert = i1 * N_KEYS + i2
        g = jax.nn.softmax(best_s, axis=-1)
        u_e = u_tab[expert]
        v_e = v_tab[expert]
        act = jax.nn.gelu(jnp.einsum('td,thkd->thk', xb, u_e,
                                     preferred_element_type=jnp.float32))
        return jnp.einsum('thk,thkd->td', (g * act).astype(xb.dtype), v_e)

    return lax.map(one_block, blocks).reshape(b, s, d)

def setup_inputs(seed: int = 0) -> dict:
    key = jax.random.key(seed)
    ks = jax.random.split(key, 24)
    f32 = jnp.float32
    NA, NR, W = N_ATTN_LAYERS, N_REC_LAYERS, LRU_WIDTH
    nrm = lambda k, shp, sc: jax.random.normal(k, shp, f32) * sc
    x = jax.random.normal(ks[0], (BATCH, SEQ, D_MODEL), f32)
    attn_norm_g = 1.0 + nrm(ks[1], (NA, D_MODEL), 0.05)
    attn_w_qkv = nrm(ks[2], (NA, D_MODEL, 3 * D_MODEL), D_MODEL ** -0.5)
    attn_q_g = 1.0 + nrm(ks[3], (NA, HEAD_DIM), 0.05)
    attn_k_g = 1.0 + nrm(ks[4], (NA, HEAD_DIM), 0.05)
    attn_rel_bias = nrm(ks[5], (NA, ATTN_HEADS, N_REL), 0.2)
    attn_w_out = nrm(ks[6], (NA, D_MODEL, D_MODEL), D_MODEL ** -0.5)
    rec_norm_g = 1.0 + nrm(ks[7], (NR, D_MODEL), 0.05)
    rec_w_in = nrm(ks[8], (NR, D_MODEL, 2 * W), D_MODEL ** -0.5)
    rec_conv_w = nrm(ks[9], (NR, CONV_WIDTH, W), CONV_WIDTH ** -0.5)
    rec_conv_b = nrm(ks[10], (NR, W), 0.02)
    rec_w_a = nrm(ks[11], (NR, LRU_HEADS, LRU_BLOCK, LRU_BLOCK), LRU_BLOCK ** -0.5)
    rec_b_a = nrm(ks[12], (NR, W), 0.02)
    rec_w_x = nrm(ks[13], (NR, LRU_HEADS, LRU_BLOCK, LRU_BLOCK), LRU_BLOCK ** -0.5)
    rec_b_x = nrm(ks[14], (NR, W), 0.02)
    a0 = jax.random.uniform(ks[15], (NR, W), f32, minval=0.9, maxval=0.999)
    base = a0 ** (1.0 / LRU_C)
    rec_lambda = jnp.log(base) - jnp.log1p(-base)
    rec_w_out = nrm(ks[16], (NR, W, D_MODEL), W ** -0.5)
    ffn_norm_g = 1.0 + nrm(ks[17], (DEPTH, D_MODEL), 0.05)
    peer_w_q = nrm(ks[18], (DEPTH, D_MODEL, PEER_HEADS * D_KEY), D_MODEL ** -0.5)
    peer_sub_keys = nrm(ks[19], (DEPTH, 2, N_KEYS, D_HALF), D_HALF ** -0.5)
    peer_u = nrm(ks[20], (DEPTH, N_EXPERTS, D_MODEL), D_MODEL ** -0.5)
    peer_v = nrm(ks[21], (DEPTH, N_EXPERTS, D_MODEL), D_MODEL ** -0.5)
    return {"x": x, "attn_norm_g": attn_norm_g, "attn_w_qkv": attn_w_qkv,
            "attn_q_g": attn_q_g, "attn_k_g": attn_k_g, "attn_rel_bias": attn_rel_bias,
            "attn_w_out": attn_w_out, "rec_norm_g": rec_norm_g, "rec_w_in": rec_w_in,
            "rec_conv_w": rec_conv_w, "rec_conv_b": rec_conv_b, "rec_w_a": rec_w_a,
            "rec_b_a": rec_b_a, "rec_w_x": rec_w_x, "rec_b_x": rec_b_x,
            "rec_lambda": rec_lambda, "rec_w_out": rec_w_out, "ffn_norm_g": ffn_norm_g,
            "peer_w_q": peer_w_q, "peer_sub_keys": peer_sub_keys,
            "peer_u": peer_u, "peer_v": peer_v}

def reference(x, attn_norm_g, attn_w_qkv, attn_q_g, attn_k_g, attn_rel_bias, attn_w_out,
              rec_norm_g, rec_w_in, rec_conv_w, rec_conv_b, rec_w_a, rec_b_a, rec_w_x,
              rec_b_x, rec_lambda, rec_w_out, ffn_norm_g, peer_w_q, peer_sub_keys,
              peer_u, peer_v):
    for layer in range(DEPTH):
        j = layer // N_MIXERS
        if layer % N_MIXERS == 0:
            x = x + chunk_attention(rms_norm(x, attn_norm_g[j]), attn_w_qkv[j], attn_q_g[j],
                                    attn_k_g[j], attn_rel_bias[j], attn_w_out[j])
        else:
            x = x + rglru_mixer(rms_norm(x, rec_norm_g[j]), rec_w_in[j], rec_conv_w[j],
                                rec_conv_b[j], rec_w_a[j], rec_b_a[j], rec_w_x[j], rec_b_x[j],
                                rec_lambda[j], rec_w_out[j])
        x = x + peer_ffn(rms_norm(x, ffn_norm_g[layer]), peer_w_q[layer], peer_sub_keys[layer],
                         peer_u[layer], peer_v[layer])
    return x


_drawn_inputs = setup_inputs


def setup_inputs(seed=0):
    import zlib

    import numpy as np

    out = dict(_drawn_inputs(seed))
    spreads = {}
    factors = {'attn_norm_g': 3.328,
     'attn_q_g': 6.174,
     'attn_k_g': 7.699,
     'rec_b_a': 26.443,
     'rec_b_x': 8.0,
     'ffn_norm_g': 8.0,
     'peer_w_q': 2.696,
     'peer_sub_keys': 2.686,
     'peer_u': 2.985,
     'peer_v': 2.701}
    for name, (base, spread) in spreads.items():
        noise = np.random.default_rng([zlib.crc32(name.encode()), seed]).standard_normal(out[name].shape)
        drawn = base * np.exp(spread * noise) if base else spread * noise
        out[name] = __import__('jax').numpy.asarray(drawn.astype(out[name].dtype))
    for name, factor in factors.items():
        out[name] = (out[name] * factor).astype(out[name].dtype)
    return out
```

```python
from contextlib import ExitStack

import concourse.bass as bass
from concourse import mybir

F32 = mybir.dt.float32
F32R = mybir.dt.float32r
U32 = mybir.dt.uint32
ALU = mybir.AluOpType
ACT = mybir.ActivationFunctionType
AX = mybir.AxisListType.X

P = 128
SEQ = 256
D = 1024
TB = SEQ // P
KC = D // P
BANK = 512
EPS = 1e-6

HEADS = 16
HD = D // HEADS
CHUNK = 64
NEG = -1e30
QKV_GROUPS = 3 * D // BANK

PHEADS = 8
TOPK = 16
NKEYS = 128
TILES = NKEYS
RAW_SLOTS = 4
HI_SLOTS = 4
LO_SLOTS = 2
UNROLL = 4
GROUP = 4
NGROUPS = SEQ // GROUP
W_SLOTS = 4

LRU_HEADS = 4
CONV = 4
LRU_C = 8.0
LOG1P_TERMS = 9

ACT_COLS = NKEYS * SEQ
A_BIAS, A_S, A_P, A_PT, A_O = 0, 4096, 6144, 8192, 10240
A_QT, A_KT, A_WOUT, A_QKV = 12288, 14336, 16384, 24576
X_NORM = 30720
P_WQ, P_QT, P_TOP, P_S = 0, 16384, 26624, 28672
R_WIN, R_GATE, R_UPAD, R_UC, R_WA, R_WX = 0, 16384, 18432, 20544, 22592, 24640
R_R, R_I, R_A, R_TH, R_WOUT = 0, 2048, 4096, 6144, 8192
UPAD = SEQ + CONV


class Count:

    def __init__(self, sem):
        self.sem, self.n = sem, 0

    def up(self, ins):
        ins.then_inc(self.sem, 1)
        self.n += 1
        return self.n


def trunk(nc, x_in, norm_g, w_qkv, qk_g, rel_rows, w_out, w_in, rec_p, w_ax, rec_w_out, w_q,
          keys_t, u_t, v_t, out):
    ctx = ExitStack()
    with ctx:
        def sb(name, shape, dt=F32):
            return ctx.enter_context(nc.sbuf_tensor(name, shape, dt))

        def sem(name):
            return ctx.enter_context(nc.semaphore(name))

        big = sb("big", [P, ACT_COLS])
        x = sb("x", [P, TB, D])
        hT = sb("hT", [P, KC, SEQ])
        h_hi = sb("h_hi", [P, KC * SEQ], F32R)
        h_lo = sb("h_lo", [P, KC * SEQ], F32R)
        raw = sb("raw", [P, RAW_SLOTS, D])
        t_hi = sb("t_hi", [P, HI_SLOTS, D], F32R)
        t_lo = sb("t_lo", [P, LO_SLOTS, D], F32R)
        slotT = sb("slotT", [P, 3, SEQ])
        keys = sb("keys", [P, 2, 2, NKEYS])
        iota = sb("iota", [P, NKEYS])
        ident = sb("ident", [P, P])
        gains = sb("gains", [P, 4, KC])
        qkg = sb("qkg", [P, 2])
        recp = sb("recp", [P, KC, 8])
        stat = sb("stat", [P, 8])
        qstat = sb("qstat", [P, TB, 32])
        smax = sb("smax", [P, 2, 4])
        ssum = sb("ssum", [P, 2, 4])
        sinv = sb("sinv", [P, 4])
        gsum = sb("gsum", [P, 16])
        sp = sb("sp", [P, 4, KC])
        decay = sb("decay", [P, 2, KC])
        eps = sb("eps", [P, 1])
        ps = [ctx.enter_context(nc.psum_tensor(f"ps{i}", [P, BANK], F32)) for i in range(8)]

        def cols(a, n):
            return big[:, a:a + n]

        acts = big[:, :].rearrange("p (j t) -> p j t", t=SEQ)
        xn = cols(X_NORM, TB * D).rearrange("p (b d) -> p b d", b=TB)
        hTf = hT[:, :, :].rearrange("p c t -> p (c t)")
        wqkv = cols(0, QKV_GROUPS * 4096).rearrange("p (n c m) -> p n c m", n=QKV_GROUPS, c=KC)
        bias = cols(A_BIAS, 4096).rearrange("p (h j) -> p h j", h=HEADS)
        S = cols(A_S, 2048).rearrange("p (s h j) -> p s h j", s=2, h=4)
        Pr = cols(A_P, 2048).rearrange("p (s h j) -> p s h j", s=2, h=4)
        PT = cols(A_PT, 2048).rearrange("p (s b q) -> p s b q", s=2, b=8)
        O = cols(A_O, 2048).rearrange("p (b d) -> p b d", b=TB)
        QT = cols(A_QT, 2048).rearrange("p (c t) -> p c t", c=KC)
        KT = cols(A_KT, 2048).rearrange("p (c t) -> p c t", c=KC)
        wo = cols(A_WOUT, 8192).rearrange("p (c m) -> p c m", c=KC)
        qkv = cols(A_QKV, 6144).rearrange("p (b m) -> p b m", b=TB)
        wq = cols(P_WQ, 16384).rearrange("p (n c m) -> p n c m", n=4, c=KC)
        qT = cols(P_QT, 1024).rearrange("p (s k t) -> p s k t", s=2, k=2)
        s_sb = cols(P_S, 4096).rearrange("p (h b k n) -> p h b k n", h=PHEADS, b=TB, k=2)
        topv = cols(P_TOP, 512).rearrange("p (b h k j) -> p b h k j", b=TB, h=PHEADS, k=2)
        topi = cols(P_TOP + 512, 512).bitcast(U32).rearrange("p (b h k j) -> p b h k j", b=TB, h=PHEADS, k=2)
        bestv = cols(P_TOP + 1024, 256).rearrange("p (b h j) -> p b h j", b=TB, h=PHEADS)
        besti = cols(P_TOP + 1280, 256).bitcast(U32).rearrange("p (b h j) -> p b h j", b=TB, h=PHEADS)
        cand = cols(P_TOP + 1536, 512).rearrange("p (b c) -> p b c", b=TB)
        hit = hTf[:, 0:512].rearrange("p (k j) -> p k j", j=TOPK)
        half_u = hTf[:, 512:768].bitcast(U32).rearrange("p (k m) -> p k m", k=2)
        half_f = hTf[:, 768:1024].rearrange("p (k m) -> p k m", k=2)
        topf = hTf[:, 1024:1280].rearrange("p (h k j) -> p h k j", h=PHEADS, k=2)
        slot = hTf[:, 1280:2048].rearrange("p (w b m) -> p w b m", w=3, b=TB)
        hot1 = hTf[:, 0:1024].rearrange("p (s t n) -> p s t n", s=2, t=GROUP)
        hot2 = hTf[:, 1024:2048].rearrange("p (s t n) -> p s t n", s=2, t=GROUP)
        w_hi = h_hi[:, 0:W_SLOTS * SEQ].rearrange("p (s t) -> p s t", s=W_SLOTS)
        w_lo = h_lo[:, 0:W_SLOTS * SEQ].rearrange("p (s t) -> p s t", s=W_SLOTS)
        win = cols(R_WIN, 16384).rearrange("p (n c m) -> p n c m", n=4, c=KC)
        gate = cols(R_GATE, 2048).rearrange("p (c t) -> p c t", c=KC)
        upad = cols(R_UPAD, KC * UPAD).rearrange("p (c t) -> p c t", c=KC)
        uc = cols(R_UC, 2048).rearrange("p (c t) -> p c t", c=KC)
        wax = cols(R_WA, 4096).rearrange("p (g h c m) -> p g h c m", g=2, h=LRU_HEADS, c=2)
        rg = cols(R_R, 4096).rearrange("p (g c t) -> p g c t", g=2, c=KC)
        ra = cols(R_A, 2048).rearrange("p (c t) -> p c t", c=KC)
        th = cols(R_TH, 2048).rearrange("p (c t) -> p c t", c=KC)
        wro = cols(R_WOUT, 8192).rearrange("p (c m) -> p c m", c=KC)

        x_in_sem = sem("x_loaded")
        small_loaded = sem("small_loaded")
        wqkv_loaded = [sem(f"wqkv_loaded{n}") for n in range(QKV_GROUPS)]
        bias_loaded, wo_loaded, wax_loaded, wro_loaded = map(sem, ("bias_loaded", "wo_loaded", "wax_loaded", "wro_loaded"))
        wq_loaded = [sem(f"wq_loaded{n}") for n in range(4)]
        win_loaded = [sem(f"win_loaded{n}") for n in range(4)]
        raw_loaded = [sem(f"raw_loaded{n}") for n in range(RAW_SLOTS)]
        stored = sem("stored")
        consts_set, const_step = sem("consts_set"), sem("const_step")
        ss_ready, rms_ready, xn_ready = sem("ss_ready"), sem("rms_ready"), sem("xn_ready")
        ht_psum, ht_by_dve, ht_by_act = sem("ht_psum"), sem("ht_by_dve"), sem("ht_by_act")
        hi_split, lo_split = sem("h_hi_ready"), sem("h_lo_ready")
        qkv_psum, qkv_copied = sem("qkv_psum"), sem("qkv_copied")
        qss_ready, qrms_ready, qn_ready = sem("qss_ready"), sem("qrms_ready"), sem("qn_ready")
        qk_psum, q_turned, k_turned = sem("qk_psum"), sem("q_turned"), sem("k_turned")
        masked, sc_psum, sc_ready, sc_max = sem("masked"), sem("sc_psum"), sem("sc_ready"), sem("sc_max")
        probs_ready, pt_psum, pt_ready = sem("probs_ready"), sem("pt_psum"), sem("pt_ready")
        pv_psum, o_ready = sem("pv_psum"), sem("o_ready")
        ot_psum, ot_by_dve, ot_by_act = sem("ot_psum"), sem("ot_by_dve"), sem("ot_by_act")
        proj_psum, x_added = sem("proj_psum"), sem("x_added")
        q_psum, q_copied, s_psum, s_copied = sem("q_psum"), sem("q_copied"), sem("s_psum"), sem("s_copied")
        topk_done, logits_ready, exp_ready, slots_ready = sem("topk_done"), sem("logits_ready"), sem("exp_ready"), sem("slots_ready")
        slot_psum, slotT_ready = sem("slot_psum"), sem("slotT_ready")
        hi_ready, lo_ready, tile_used = sem("tile_hi_ready"), sem("tile_lo_ready"), sem("tile_used")
        act_ready = sem("act_ready")
        hot_ready, gates_psum, gated = sem("hot_ready"), sem("gates_psum"), sem("gated")
        whi_ready, wlo_ready, x_stored = sem("whi_ready"), sem("wlo_ready"), sem("x_replaced")
        lam_exp, abs_ready = sem("lam_exp"), sem("abs_ready")
        rec_psum, rec_copied, conv_done = sem("rec_psum"), sem("rec_copied"), sem("conv_done")
        rg_psum, rg_ready, ra_ready, one_minus, mult_ready, y_ready = map(
            sem, ("rg_psum", "rg_ready", "decay_ready", "variance_ready", "mult_ready", "y_ready"))
        dve_step, act_step = sem("dve_step"), sem("act_step")

        block = ctx.enter_context(nc.Block())

        @block.sync
        def _(sp_):
            def slab(dst, w, n):
                return dst, w.rearrange("(c p) m -> p c m", p=P)[:, :, n * BANK:(n + 1) * BANK]

            def stream(table, base):
                with sp_.Fori(0, TILES // UNROLL) as g:
                    for k in range(UNROLL):
                        sp_.wait_ge(lo_ready, g * UNROLL + (base + k + 1))
                        sp_.dma_start(raw[:, k, :], table[g * UNROLL + k]).then_inc(raw_loaded[k], 16)

            sp_.dma_start(x[:, :, :], x_in.rearrange("(b p) d -> p b d", p=P)).then_inc(x_in_sem, 16)
            for dst, src in ((gains[:, :, :], norm_g), (qkg[:, :], qk_g), (recp[:, :, :], rec_p), (keys[:, :, :, :], keys_t)):
                sp_.dma_start(dst, src).then_inc(small_loaded, 16)
            for n in range(QKV_GROUPS):
                sp_.dma_start(*slab(wqkv[:, n], w_qkv, n)).then_inc(wqkv_loaded[n], 16)
            sp_.wait_ge(qkv_psum, 2)
            row = 2 * CHUNK + CHUNK
            for a, b, n in ((0, CHUNK, row), (CHUNK, P, 2 * P)):
                sp_.dma_start(bias[a:b, :, 0:n], rel_rows[a:b, :, 0:n]).then_inc(bias_loaded, 16)
            sp_.wait_ge(qkv_psum, 2 * QKV_GROUPS)
            sp_.dma_start(wo, w_out.rearrange("(c p) m -> p c m", p=P)).then_inc(wo_loaded, 16)
            for l in range(2):
                if l == 0:
                    sp_.wait_ge(o_ready, 8)
                    sp_.wait_ge(ot_psum, 4)
                else:
                    sp_.wait_ge(y_ready, KC)
                for n in range(4):
                    if l == 1 and n == 2:
                        sp_.wait_ge(proj_psum, 8)
                    sp_.dma_start(*slab(wq[:, n], w_q[l], n)).then_inc(wq_loaded[n], 16)
                stream(u_t[l], l * 2 * TILES)
                stream(v_t[l], l * 2 * TILES + TILES)
                if l == 0:
                    sp_.wait_ge(wlo_ready, TILES)
                    for n in (2, 3, 0, 1):
                        sp_.dma_start(*slab(win[:, n], w_in, n)).then_inc(win_loaded[n], 16)
                    sp_.dma_start(wax, w_ax).then_inc(wax_loaded, 16)
                    sp_.wait_ge(rec_psum, 8)
                    sp_.dma_start(wro, rec_w_out.rearrange("(c p) m -> p c m", p=P)).then_inc(wro_loaded, 16)
            sp_.wait_ge(x_stored, 8)
            sp_.dma_start(out.rearrange("(b p) d -> p b d", p=P), x[:, :, :]).then_inc(stored, 16)
            sp_.wait_ge(stored, 16)

        @block.gpsimd
        def _(pool):
            pool.iota(iota[:, :], pattern=[[1, NKEYS]], base=0, channel_multiplier=0,
                      allow_small_or_imprecise_dtypes=True).then_inc(consts_set, 1)
            pool.memset(ident[:, :], 0.0).then_inc(const_step, 1)
            pool.wait_ge(const_step, 1)
            pool.affine_select(out=ident[:, :], in_=ident[:, :], compare_op=ALU.not_equal, fill=1.0, base=0,
                               pattern=[[-1, P]], channel_multiplier=1).then_inc(consts_set, 1)
            for _ in range(RAW_SLOTS):
                pool.sem_inc(lo_ready, 1)

            def lo_parts(base):
                with pool.Fori(0, TILES // UNROLL) as g:
                    for k in range(UNROLL):
                        pool.wait_ge(tile_used, g * UNROLL + (base + k + 1 + HI_SLOTS - LO_SLOTS))
                        pool.wait_ge(hi_ready, g * UNROLL + (base + k + 1))
                        pool.tensor_tensor(t_lo[:, k % LO_SLOTS, :], raw[:, k, :], t_hi[:, k, :].bitcast(F32),
                                           ALU.subtract).then_inc(lo_ready, 1)

            for l in range(2):
                lo_parts(l * 2 * TILES)
                lo_parts(l * 2 * TILES + TILES)

        @block.scalar
        def _(act):
            def turned(n):
                for c in range(KC // 2, KC):
                    act.wait_ge(ht_psum, 4 * n + c // 2 + 1)
                    act.activation(hT[:, c, :], ps[c // 2][:, (c % 2) * SEQ:(c % 2 + 1) * SEQ], ACT.Copy,
                                   scale=gains[:, n, c:c + 1]).then_inc(ht_by_act, 1)

            def norm(n):
                act.wait_ge(ss_ready, n + 1)
                act.activation(stat[:, 2:4], stat[:, 0:2], ACT.Sqrt, bias=eps[:, :], scale=1.0 / D).then_inc(rms_ready, 1)
                turned(n)

            def hi_part(g, k, base):
                act.wait_ge(tile_used, g * UNROLL + (base + k + 1))
                act.wait_ge(raw_loaded[k], g * 16 + 16 * (base // UNROLL + 1))
                act.activation(t_hi[:, k, :], raw[:, k, :], ACT.Copy).then_inc(hi_ready, 1)

            def attention():
                for n in range(QKV_GROUPS):
                    for b in range(TB):
                        i = 2 * n + b
                        act.wait_ge(qkv_psum, i + 1)
                        act.activation(qkv[:, b, n * BANK:(n + 1) * BANK], ps[4 + i % 4][:, :], ACT.Copy).then_inc(qkv_copied, 1)
                        if n == 5:
                            act.wait_ge(qss_ready, b + 1)
                            act.activation(qstat[:, b, :], qstat[:, b, :], ACT.Sqrt, bias=eps[:, :],
                                           scale=1.0 / HD).then_inc(qrms_ready, 1)
                for b in range(TB):
                    for m in range(2):
                        i = b * 4 + 2 + m
                        act.wait_ge(qk_psum, i + 1)
                        act.activation(KT[:, 4 * m:4 * m + 4, b * P:(b + 1) * P],
                                       ps[i % 4][:, :].rearrange("p (c t) -> p c t", c=4), ACT.Copy,
                                       scale=qkg[:, 1:2]).then_inc(k_turned, 1)
                for s in range(8):
                    nb = 1 + s // 4
                    act.wait_ge(sc_max, s + 1)
                    if s >= 2:
                        act.wait_ge(pt_psum, s - 1)
                        act.wait_ge(o_ready, s - 1)
                    for h in range(4):
                        act.activation(Pr[:, s % 2, h, 0:nb * P], S[:, s % 2, h, 0:nb * P], ACT.Exp,
                                       bias=smax[:, s % 2, h:h + 1], accum_out=ssum[:, s % 2, h:h + 1]).then_inc(probs_ready, 1)
                    act.wait_ge(pt_psum, s + 1)
                    if s >= 2:
                        act.wait_ge(pv_psum, s - 1)
                    for m in range(nb):
                        act.activation(PT[:, s % 2, 4 * m:4 * m + 4, :], ps[4 + m][:, :].rearrange("p (b q) -> p b q", b=4),
                                       ACT.Copy).then_inc(pt_ready, 1)
                for m in (2, 3):
                    act.wait_ge(ot_psum, m + 1)
                    act.activation(hT[:, 2 * m:2 * m + 2, :], ps[m][:, :].rearrange("p (c t) -> p c t", c=2), ACT.Copy).then_inc(ot_by_act, 1)

            def peer(l):
                n = 2 * l + 1
                norm(n)
                act.wait_ge(ht_by_dve, 4 * (n + 1))
                act.wait_ge(ht_by_act, 4 * (n + 1))
                act.activation(h_hi[:, :], hTf, ACT.Copy).then_inc(hi_split, 1)
                for h in range(PHEADS):
                    act.wait_ge(q_psum, l * PHEADS + h + 1)
                    if h >= 2:
                        act.wait_ge(s_psum, l * PHEADS + h - 1)
                    act.activation(qT[:, h % 2], ps[4 + h % 2][:, :].rearrange("p (k t) -> p k t", k=2), ACT.Copy).then_inc(q_copied, 1)
                    if h >= 1:
                        act.wait_ge(s_psum, l * PHEADS + h)
                        act.activation(s_sb[:, h - 1].rearrange("p b k n -> p (b k n)"), ps[6 + (h - 1) % 2][:, :], ACT.Copy).then_inc(s_copied, 1)
                act.wait_ge(s_psum, (l + 1) * PHEADS)
                act.activation(s_sb[:, PHEADS - 1].rearrange("p b k n -> p (b k n)"), ps[6 + (PHEADS - 1) % 2][:, :], ACT.Copy).then_inc(s_copied, 1)

                base = l * 2 * TILES
                for k in range(UNROLL):
                    hi_part(0, k, base)

                def gelu(g, k):
                    act.wait_ge(tile_used, g * UNROLL + (base + k + 1 + HI_SLOTS))
                    act.activation(big[:, bass.ds((g * UNROLL + k - 1) * SEQ, 2 * SEQ)], ps[k // 2][:, :],
                                   ACT.Gelu_apprx_tanh).then_inc(act_ready, 1)

                first = P_TOP // SEQ // UNROLL
                for a, b in ((0, first), (first, TILES // UNROLL)):
                    if a:
                        act.wait_ge(logits_ready, l + 1)
                    with act.Fori(a, b) as g:
                        for k in range(UNROLL):
                            hi_part(g, k, base + UNROLL)
                            if k % 2:
                                gelu(g, k)
                act.activation(slot[:, 2], slot[:, 2], ACT.Exp).then_inc(exp_ready, 1)
                with act.Fori(0, TILES // UNROLL - 1) as g:
                    for k in range(UNROLL):
                        hi_part(g, k, base + TILES + UNROLL)

            def recurrent():
                norm(2)
                for i in range(8):
                    act.wait_ge(rec_psum, i + 1)
                    src = ps[4 + i % 4][:, :].rearrange("p (c t) -> p c t", c=2)
                    if i < 4:
                        act.activation(upad[:, 2 * i:2 * i + 2, CONV - 1:CONV - 1 + SEQ], src, ACT.Copy).then_inc(rec_copied, 1)
                    else:
                        act.activation(gate[:, 2 * i - 8:2 * i - 6, :], src, ACT.Gelu_apprx_tanh).then_inc(rec_copied, 1)
                for i in range(8):
                    h, g = i // 2, i % 2
                    act.wait_ge(rg_psum, i + 1)
                    for c in range(2):
                        act.activation(rg[:, g, 2 * h + c, :], ps[i % 4][:, c * SEQ:(c + 1) * SEQ], ACT.Sigmoid,
                                       bias=recp[:, 2 * h + c, 5 + g:6 + g]).then_inc(rg_ready, 1)
                act.wait_ge(rg_ready, 16)
                for c in range(KC):
                    act.activation(th[:, c, :], rg[:, 0, c, :], ACT.Tanh, scale=decay[:, 1, c:c + 1]).then_inc(ra_ready, 1)
                for c in range(KC):
                    act.activation(ra[:, c, :], rg[:, 0, c, :], ACT.Exp, scale=decay[:, 0, c:c + 1]).then_inc(ra_ready, 1)
                act.wait_ge(one_minus, 1)
                act.activation(th, th, ACT.Sqrt).then_inc(mult_ready, 1)

            for _ in range(2):
                act.sem_inc(act_ready, 1)
            act.wait_ge(small_loaded, 64)
            act.activation(sp[:, 0, :], recp[:, :, 7], ACT.Abs).then_inc(abs_ready, 1)
            act.wait_ge(abs_ready, 1)
            act.activation(sp[:, 1, :], sp[:, 0, :], ACT.Exp, scale=-1.0).then_inc(lam_exp, 1)
            norm(0)
            attention()
            peer(0)
            recurrent()
            peer(1)

        @block.vector
        def _(dve):
            step = Count(dve_step)

            def link(ins):
                dve.wait_ge(step.sem, step.up(ins))

            def norm(n):
                for b in range(TB):
                    ins = dve.tensor_tensor_reduce(xn[:, b, :], x[:, b, :], x[:, b, :], 1.0, 0.0, ALU.mult, ALU.add, stat[:, b:b + 1])
                    if b == 0:
                        link(ins)
                ins.then_inc(ss_ready, 1)
                dve.wait_ge(rms_ready, n + 1)
                link(dve.reciprocal(stat[:, 4:6], stat[:, 2:4]))
                for b in range(TB):
                    dve.tensor_scalar(xn[:, b, :], x[:, b, :], stat[:, 4 + b:5 + b], None, ALU.mult).then_inc(xn_ready, 1)
                for c in range(KC // 2):
                    dve.wait_ge(ht_psum, 4 * n + c // 2 + 1)
                    dve.tensor_scalar(hT[:, c, :], ps[c // 2][:, (c % 2) * SEQ:(c % 2 + 1) * SEQ], gains[:, n, c:c + 1], None,
                                      ALU.mult).then_inc(ht_by_dve, 1)

            def add_projection(m):
                for i in range(4):
                    b, n = i // 2, i % 2
                    dve.wait_ge(proj_psum, 4 * m + i + 1)
                    xs = x[:, b, n * BANK:(n + 1) * BANK]
                    dve.tensor_tensor(xs, xs, ps[4 + i][:, :], ALU.add).then_inc(x_added, 1)
                dve.wait_ge(x_added, 4 * (m + 1))

            def attention():
                dve.wait_ge(qkv_psum, 12)
                sq = cols(A_S, 2048)
                for b in range(TB):
                    dve.wait_ge(qkv_copied, 8)
                    qk = qkv[:, b, 0:2 * D]
                    link(dve.tensor_tensor(sq, qk, qk, ALU.mult))
                    dve.tensor_reduce(qstat[:, b, :], sq.rearrange("p (h d) -> p h d", d=HD), AX, ALU.add).then_inc(qss_ready, 1)
                    dve.wait_ge(qss_ready, b + 1)
                for b in range(TB):
                    dve.wait_ge(qrms_ready, b + 1)
                    link(dve.reciprocal(qstat[:, b, :], qstat[:, b, :]))
                    qk = qkv[:, b, 0:2 * D].rearrange("p (h d) -> p h d", d=HD)
                    dve.tensor_tensor(qk, qk, qstat[:, b, :].unsqueeze(2).to_broadcast([P, 32, HD]), ALU.mult).then_inc(qn_ready, 1)
                dve.memset(bias[0:CHUNK, :, 3 * CHUNK:4 * CHUNK], NEG).then_inc(masked, 1)
                for b in range(TB):
                    for m in range(2):
                        i = b * 4 + m
                        dve.wait_ge(qk_psum, i + 1)
                        dve.tensor_scalar(QT[:, 4 * m:4 * m + 4, b * P:(b + 1) * P],
                                          ps[i % 4][:, :].rearrange("p (c t) -> p c t", c=4), qkg[:, 0:1], None,
                                          ALU.mult).then_inc(q_turned, 1)
                dve.wait_ge(bias_loaded, 32)
                dve.wait_ge(masked, 1)

                def scores(s):
                    b, g = s // 4, s % 4
                    w = (b + 1) * P
                    dve.wait_ge(sc_psum, s + 1)
                    if s >= 2:
                        dve.wait_ge(probs_ready, 4 * (s - 1))
                    for r in range(2):
                        dve.scalar_tensor_tensor(
                            out=S[:, s % 2, r:4:2, 0:w], in0=ps[2 * (s % 2) + r][:, :].rearrange("p (m j) -> p m j", m=2)[:, :, 0:w],
                            scalar=HD ** -0.5, in1=bias[:, 4 * g + r:4 * g + 4:2, 2 * P - w:2 * P], op0=ALU.mult,
                            op1=ALU.add).then_inc(sc_ready, 1)
                    dve.wait_ge(sc_ready, 2 * (s + 1))
                    dve.tensor_reduce(smax[:, s % 2, :], S[:, s % 2, :, 0:w], AX, ALU.max, negate=True).then_inc(sc_max, 1)

                def outputs(s):
                    b, g = s // 4, s % 4
                    dve.wait_ge(probs_ready, 4 * (s + 1))
                    link(dve.reciprocal(sinv[:, :], ssum[:, s % 2, :]))
                    dve.wait_ge(pv_psum, s + 1)
                    dve.tensor_tensor(O[:, b, g * 4 * HD:(g + 1) * 4 * HD].rearrange("p (h d) -> p h d", h=4),
                                      ps[6 + s % 2][:, 0:4 * HD].rearrange("p (h d) -> p h d", h=4),
                                      sinv[:, :].unsqueeze(2).to_broadcast([P, 4, HD]), ALU.mult).then_inc(o_ready, 1)
                    dve.wait_ge(o_ready, s + 1)

                scores(0)
                for s in range(8):
                    if s < 7:
                        scores(s + 1)
                    outputs(s)
                for m in (0, 1):
                    dve.wait_ge(ot_psum, m + 1)
                    dve.tensor_copy(hT[:, 2 * m:2 * m + 2, :], ps[m][:, :].rearrange("p (c t) -> p c t", c=2)).then_inc(ot_by_dve, 1)
                add_projection(0)

            def top16(values, index, source):
                for r in range(2):
                    half = slice(8 * r, 8 * r + 8)
                    for v, s in zip(values, source):
                        n = step.up(dve.max(v[:, half], s))
                    dve.wait_ge(step.sem, n)
                    for v, i, s in zip(values, index, source):
                        n = step.up(dve.max_index(i[:, half], v[:, half], s))
                    if r == 0:
                        dve.wait_ge(step.sem, n)
                        for v, s in zip(values, source):
                            n = step.up(dve.match_replace(s, v[:, half], s, -3e38))
                        dve.wait_ge(step.sem, n)

            def peer(l):
                n = 2 * l + 1
                norm(n)
                dve.wait_ge(hi_split, l + 1)
                dve.tensor_tensor(h_lo[:, :], hTf, h_hi[:, :].bitcast(F32), ALU.subtract).then_inc(lo_split, 1)
                for h in range(PHEADS):
                    dve.wait_ge(s_copied, l * PHEADS + h + 1)
                    pairs = [(b, k) for b in range(TB) for k in range(2)]
                    top16([topv[:, b, h, k, :] for b, k in pairs], [topi[:, b, h, k, :] for b, k in pairs],
                          [s_sb[:, h, b, k, :] for b, k in pairs])
                    dve.wait_ge(step.sem, step.n)
                    for b in range(TB):
                        m = step.up(dve.tensor_tensor(
                            cand[:, b, :].rearrange("p (i j) -> p i j", i=TOPK),
                            topv[:, b, h, 0, :].unsqueeze(2).to_broadcast([P, TOPK, TOPK]),
                            topv[:, b, h, 1, :].unsqueeze(1).to_broadcast([P, TOPK, TOPK]), ALU.add))
                    dve.wait_ge(step.sem, m)
                    top16([bestv[:, b, h, :] for b in range(TB)], [besti[:, b, h, :] for b in range(TB)],
                          [cand[:, b, :] for b in range(TB)])
                    dve.wait_ge(step.sem, step.n)
                dve.wait_ge(q_psum, (l + 1) * PHEADS)
                dve.wait_ge(hi_split, l + 1)
                dve.wait_ge(lo_split, l + 1)
                for b in range(TB):
                    flat = besti[:, b].rearrange("p h j -> p (h j)")
                    dve.tensor_single_scalar(half_u[:, 0, :], flat, 4, ALU.logical_shift_right)
                    link(dve.tensor_single_scalar(half_u[:, 1, :], flat, TOPK - 1, ALU.bitwise_and))
                    dve.tensor_copy(half_f, half_u)
                    link(dve.tensor_copy(topf, topi[:, b]))
                    for k in range(2):
                        for h in range(0, PHEADS, 2):
                            m = slice(h * TOPK, (h + 2) * TOPK)
                            link(dve.tensor_tensor(hit, half_f[:, k, m].unsqueeze(2).to_broadcast([P, 2 * TOPK, TOPK]),
                                                   iota[:, 0:TOPK].unsqueeze(1).to_broadcast([P, 2 * TOPK, TOPK]), ALU.is_equal))
                            hit4 = hit.rearrange("p (h k) j -> p h k j", h=2)
                            link(dve.tensor_tensor(hit4, hit4, topf[:, h:h + 2, k, :].unsqueeze(2).to_broadcast([P, 2, TOPK, TOPK]), ALU.mult))
                            link(dve.tensor_reduce(slot[:, k, b, m], hit, AX, ALU.add))
                    ins = dve.tensor_tensor(slot[:, 2, b, :].rearrange("p (h j) -> p h j", h=PHEADS), bestv[:, b],
                                            bestv[:, b, :, 0:1].to_broadcast([P, PHEADS, TOPK]), ALU.subtract)
                    if b == 0:
                        link(ins)
                ins.then_inc(logits_ready, 1)
                dve.wait_ge(exp_ready, l + 1)
                w3 = slot[:, 2].rearrange("p b (h j) -> p (b h) j", h=PHEADS)
                link(dve.tensor_reduce(gsum[:, :], w3, AX, ALU.add))
                link(dve.reciprocal(gsum[:, :], gsum[:, :]))
                dve.tensor_tensor(w3, w3, gsum[:, :].unsqueeze(2).to_broadcast([P, TB * PHEADS, TOPK]), ALU.mult).then_inc(slots_ready, 1)
                dve.wait_ge(slot_psum, l + 1)
                dve.tensor_copy(slotT[:, 0:2, :].rearrange("p w t -> p (w t)"), ps[2][:, :]).then_inc(slotT_ready, 1)
                dve.tensor_copy(slotT[:, 2, :], ps[3][:, 0:SEQ]).then_inc(slotT_ready, 1)
                dve.wait_ge(slotT_ready, 2 * (l + 1))
                dve.wait_ge(act_ready, (l + 1) * TILES // 2 + 2)

                def weighted(g, k):
                    dve.wait_ge(gates_psum, g * 4 + (l * NGROUPS + k + 1))
                    for t in range(GROUP):
                        at = g * (4 * GROUP) + (k * GROUP + t)
                        dve.tensor_scalar(hot1[:, k % 2, t, :], iota[:, :], slotT[:, 0, bass.ds(at, 1)], None, ALU.is_equal)
                        ins = dve.tensor_scalar(hot2[:, k % 2, t, :], iota[:, :], slotT[:, 1, bass.ds(at, 1)],
                                                slotT[:, 2, bass.ds(at, 1)], ALU.is_equal, ALU.mult)
                    ins.then_inc(hot_ready, 1)

                def apply(g, k):
                    dve.wait_ge(gates_psum, g * 4 + (l * NGROUPS + k + 1 + 2))
                    a = acts[:, :, bass.ds(g * (4 * GROUP) + k * GROUP, GROUP)]
                    dve.tensor_tensor(a, a, ps[k][:, :].rearrange("p (t j) -> p j t", t=GROUP), ALU.mult).then_inc(gated, 1)

                def body(g, last):
                    for k in range(4):
                        if not last or k < 3:
                            weighted(g, k + 1)
                        apply(g, k)

                weighted(0, 0)
                with dve.Fori(0, NGROUPS // 4 - 1) as g:
                    body(g, False)
                body(NGROUPS // 4 - 1, True)
                dve.wait_ge(gated, 4 + (l + 1) * NGROUPS)

                base = l * 2 * TILES + TILES
                with dve.Fori(0, TILES // UNROLL) as g:
                    for k in range(UNROLL):
                        dve.wait_ge(tile_used, g * UNROLL + (base + k + 1))
                        a = acts[:, g * UNROLL + k, :]
                        dve.tensor_copy(w_hi[:, k, :], a).then_inc(whi_ready, 1)
                        dve.wait_ge(whi_ready, g * UNROLL + (l * TILES + k + 1))
                        dve.tensor_tensor(w_lo[:, k, :], a, w_hi[:, k, :].bitcast(F32), ALU.subtract).then_inc(wlo_ready, 1)
                dve.wait_ge(tile_used, (l + 1) * 2 * TILES + HI_SLOTS)
                for i in range(4):
                    b, n = i // 2, i % 2
                    dve.tensor_copy(x[:, b, n * BANK:(n + 1) * BANK], ps[4 + i][:, :]).then_inc(x_stored, 1)
                dve.wait_ge(x_stored, 4 * (l + 1))

            def softplus():
                lam = recp[:, :, 7]
                dve.wait_ge(lam_exp, 1)
                e, z, z2, acc = (sp[:, i, :] for i in (1, 2, 3, 0))
                link(dve.tensor_scalar(z, e, 2.0, None, ALU.add))
                link(dve.reciprocal(z, z))
                link(dve.tensor_tensor(z, z, e, ALU.mult))
                link(dve.tensor_tensor(z2, z, z, ALU.mult))
                link(dve.memset(acc, 1.0 / (2 * LOG1P_TERMS + 1)))
                for n in range(LOG1P_TERMS - 1, -1, -1):
                    link(dve.tensor_tensor(acc, acc, z2, ALU.mult))
                    link(dve.tensor_scalar(acc, acc, 1.0 / (2 * n + 1), None, ALU.add))
                link(dve.tensor_tensor(acc, acc, z, ALU.mult))
                link(dve.tensor_scalar(e, lam, -1.0, 0.0, ALU.mult, ALU.max))
                link(dve.scalar_tensor_tensor(out=z, in0=acc, scalar=2.0, in1=e, op0=ALU.mult, op1=ALU.add))
                dve.tensor_scalar(decay[:, 0, :], z, -LRU_C, None, ALU.mult)
                link(dve.tensor_scalar(decay[:, 1, :], z, LRU_C, None, ALU.mult))

            def recurrent():
                norm(2)
                dve.memset(upad[:, :, 0:CONV - 1], 0.0).then_inc(dve_step, 1)
                step.n += 1
                dve.wait_ge(dve_step, step.n)
                for i in range(4):
                    dve.wait_ge(rec_copied, i + 1)
                    for k in range(CONV):
                        for c in (2 * i, 2 * i + 1):
                            src = upad[:, c, k:k + SEQ]
                            if k == 0:
                                ins = dve.tensor_scalar(uc[:, c, :], src, recp[:, c, 0:1], recp[:, c, 4:5], ALU.mult, ALU.add)
                            else:
                                ins = dve.scalar_tensor_tensor(out=uc[:, c, :], in0=src, scalar=recp[:, c, k:k + 1], in1=uc[:, c, :],
                                                               op0=ALU.mult, op1=ALU.add)
                            if k == CONV - 1:
                                ins.then_inc(conv_done, 1)
                            elif c % 2:
                                link(ins)
                dve.wait_ge(ra_ready, 16)
                dve.wait_ge(conv_done, 8)
                link(dve.tensor_tensor(rg[:, 1], rg[:, 1], uc, ALU.mult))
                link(dve.tensor_tensor(rg[:, 0], ra, ra, ALU.mult))
                dve.scalar_tensor_tensor(out=th, in0=rg[:, 0], scalar=1.0, in1=th, op0=ALU.add, op1=ALU.mult).then_inc(one_minus, 1)
                dve.wait_ge(mult_ready, 1)
                link(dve.tensor_tensor(rg[:, 1], rg[:, 1], th, ALU.mult))
                for c in range(KC):
                    ins = dve.tensor_tensor_scan(uc[:, c, :], ra[:, c, :], rg[:, 1, c, :], 0.0, ALU.mult, ALU.add)
                link(ins)
                dve.wait_ge(rec_copied, 8)
                for c in range(KC):
                    dve.tensor_tensor(hT[:, c, :], uc[:, c, :], gate[:, c, :], ALU.mult).then_inc(y_ready, 1)
                add_projection(1)

            dve.memset(eps[:, :], EPS).then_inc(consts_set, 1)
            for _ in range(4):
                dve.sem_inc(gated, 1)
            dve.wait_ge(small_loaded, 64)
            softplus()
            dve.wait_ge(x_in_sem, 16)
            norm(0)
            attention()
            peer(0)
            recurrent()
            peer(1)

        @block.tensor
        def _(pe):
            def norm(n):
                for m in range(KC // 2):
                    for c in (2 * m, 2 * m + 1):
                        for b in range(TB):
                            pe.wait_ge(xn_ready, 2 * n + b + 1)
                            a = (c % 2) * SEQ + b * P
                            ins = pe.transpose(ps[m][:, a:a + P], xn[:, b, c * P:(c + 1) * P], ident[:, :])
                    ins.then_inc(ht_psum, 1)

            def ht_is_ready(n):
                pe.wait_ge(ht_by_dve, 4 * (n + 1))
                pe.wait_ge(ht_by_act, 4 * (n + 1))

            def project(w, m):
                for i in range(4):
                    b, n = i // 2, i % 2
                    for c in range(KC):
                        ins = pe.matmul(ps[4 + i][:, :], hT[:, c, b * P:(b + 1) * P], w[:, c, n * BANK:(n + 1) * BANK],
                                        start=(c == 0), stop=(c == KC - 1))
                    ins.then_inc(proj_psum, 1)

            def attention():
                ht_is_ready(0)
                for n in range(QKV_GROUPS):
                    pe.wait_ge(wqkv_loaded[n], 16)
                    for b in range(TB):
                        i = 2 * n + b
                        if i >= 4:
                            pe.wait_ge(qkv_copied, i - 3)
                        for c in range(KC):
                            ins = pe.matmul(ps[4 + i % 4][:, :], hT[:, c, b * P:(b + 1) * P], wqkv[:, n, c, :],
                                            start=(c == 0), stop=(c == KC - 1))
                        ins.then_inc(qkv_psum, 1)
                for b in range(TB):
                    pe.wait_ge(qn_ready, b + 1)
                    for k in range(2):
                        for m in range(2):
                            i = b * 4 + k * 2 + m
                            if i >= 4:
                                pe.wait_ge((q_turned, k_turned)[k], m + 1)
                            for c in range(4):
                                a = k * D + (4 * m + c) * P
                                ins = pe.transpose(ps[i % 4][:, c * P:(c + 1) * P], qkv[:, b, a:a + P], ident[:, :])
                            ins.then_inc(qk_psum, 1)
                pe.wait_ge(q_turned, 4)
                pe.wait_ge(k_turned, 4)

                def scores(s):
                    b, g = s // 4, s % 4
                    w = (b + 1) * P
                    if s >= 2:
                        pe.wait_ge(sc_ready, 2 * (s - 1))
                    for m in range(2):
                        for r in range(2):
                            rows = slice(r * HD, (r + 1) * HD)
                            ins = pe.matmul(ps[2 * (s % 2) + r][:, m * 2 * P:m * 2 * P + w], QT[rows, 2 * g + m, b * P:(b + 1) * P],
                                            KT[rows, 2 * g + m, 0:w], start=True, stop=True)
                    ins.then_inc(sc_psum, 1)

                def weigh(s):
                    b, g = s // 4, s % 4
                    pe.wait_ge(probs_ready, 4 * (s + 1))
                    done = sum(1 + i // 4 for i in range(s))
                    if s >= 1:
                        pe.wait_ge(pt_ready, done)
                    for h in range(4):
                        for k in range(b + 1):
                            i = h * (b + 1) + k
                            ins = pe.transpose(ps[4 + i // 4][:, (i % 4) * P:(i % 4 + 1) * P], Pr[:, s % 2, h, k * P:(k + 1) * P], ident[:, :])
                    ins.then_inc(pt_psum, 1)
                    pe.wait_ge(pt_ready, done + b + 1)
                    if s >= 2:
                        pe.wait_ge(o_ready, s - 1)
                    for h in range(4):
                        for k in range(b + 1):
                            a = 2 * D + (4 * g + h) * HD
                            ins = pe.matmul(ps[6 + s % 2][:, h * HD:(h + 1) * HD], PT[:, s % 2, h * (b + 1) + k, :], qkv[:, k, a:a + HD],
                                            start=(k == 0), stop=(k == b))
                    ins.then_inc(pv_psum, 1)

                scores(0)
                for s in range(8):
                    if s < 7:
                        scores(s + 1)
                    weigh(s)
                pe.wait_ge(o_ready, 8)
                for m in range(KC // 2):
                    for c in (2 * m, 2 * m + 1):
                        for b in range(TB):
                            a = (c % 2) * SEQ + b * P
                            ins = pe.transpose(ps[m][:, a:a + P], O[:, b, c * P:(c + 1) * P], ident[:, :])
                    ins.then_inc(ot_psum, 1)
                pe.wait_ge(ot_by_dve, 2)
                pe.wait_ge(ot_by_act, 2)
                pe.wait_ge(wo_loaded, 16)
                project(wo, 0)

            def peer(l):
                n = 2 * l + 1
                norm(n)
                ht_is_ready(n)

                def key_scores(h):
                    pe.wait_ge(q_copied, l * PHEADS + h + 1)
                    if h >= 2:
                        pe.wait_ge(s_copied, l * PHEADS + h - 1)
                    for b in range(TB):
                        for k in range(2):
                            a = (2 * b + k) * NKEYS
                            ins = pe.matmul(ps[6 + h % 2][:, a:a + NKEYS], qT[:, h % 2, k, b * P:(b + 1) * P], keys[:, l, k, :],
                                            start=True, stop=True)
                    ins.then_inc(s_psum, 1)

                if l == 0:
                    pe.wait_ge(x_added, 4)
                else:
                    pe.wait_ge(x_added, 8)
                for h in range(PHEADS):
                    pe.wait_ge(wq_loaded[h // 2], 16 * (l + 1))
                    if h >= 2:
                        pe.wait_ge(q_copied, l * PHEADS + h - 1)
                    for k in range(2):
                        for c in range(KC):
                            a = (h % 2) * 2 * P + k * P
                            ins = pe.matmul(ps[4 + h % 2][:, k * SEQ:(k + 1) * SEQ], wq[:, h // 2, c, a:a + P], hT[:, c, :],
                                            start=(c == 0), stop=(c == KC - 1))
                    ins.then_inc(q_psum, 1)
                    if h >= 1:
                        key_scores(h - 1)
                key_scores(PHEADS - 1)

                pe.wait_ge(lo_split, l + 1)
                base = l * 2 * TILES
                with pe.Fori(0, TILES // UNROLL) as g:
                    for k in range(UNROLL):
                        if k % 2 == 0:
                            pe.wait_ge(act_ready, g * 2 + (l * TILES // 2 + k // 2 + 1))
                        pe.wait_ge(hi_ready, g * UNROLL + (base + k + 1))
                        pe.wait_ge(lo_ready, g * UNROLL + (base + k + 1 + RAW_SLOTS))
                        o = ps[k // 2][:, (k % 2) * SEQ:(k % 2 + 1) * SEQ]
                        for c in range(KC):
                            hi = t_hi[:, k, c * P:(c + 1) * P]
                            lo = t_lo[:, k % LO_SLOTS, c * P:(c + 1) * P]
                            m = slice(c * SEQ, (c + 1) * SEQ)
                            pe.matmul(o, hi, h_hi[:, m], start=(c == 0), stop=False)
                            pe.matmul(o, hi, h_lo[:, m], start=False, stop=False)
                            ins = pe.matmul(o, lo, h_hi[:, m], start=False, stop=(c == KC - 1))
                        ins.then_inc(tile_used, 1)

                pe.wait_ge(slots_ready, l + 1)
                for w in range(3):
                    for b in range(TB):
                        a = (w % 2) * SEQ + b * P
                        ins = pe.transpose(ps[2 + w // 2][:, a:a + P], slot[:, w, b, :], ident[:, :])
                ins.then_inc(slot_psum, 1)

                with pe.Fori(0, NGROUPS // 4) as g:
                    for k in range(4):
                        pe.wait_ge(hot_ready, g * 4 + (l * NGROUPS + k + 1))
                        pe.wait_ge(gated, g * 4 + (l * NGROUPS + k + 1))
                        for t in range(GROUP):
                            ins = pe.matmul(ps[k][:, t * NKEYS:(t + 1) * NKEYS], hot1[:, k % 2, t, :], hot2[:, k % 2, t, :],
                                            start=True, stop=True)
                        ins.then_inc(gates_psum, 1)

                for i in range(4):
                    b, n = i // 2, i % 2
                    pe.matmul(ps[4 + i][:, :], ident[:, :], x[:, b, n * BANK:(n + 1) * BANK], start=True, stop=False, skip_group_check=True)
                with pe.Fori(0, TILES // UNROLL) as g:
                    for k in range(UNROLL):
                        pe.wait_ge(hi_ready, g * UNROLL + (base + TILES + k + 1))
                        pe.wait_ge(lo_ready, g * UNROLL + (base + TILES + k + 1 + RAW_SLOTS))
                        pe.wait_ge(wlo_ready, g * UNROLL + (l * TILES + k + 1))
                        for b in range(TB):
                            for w, v in ((w_hi[:, k], t_hi[:, k]), (w_hi[:, k], t_lo[:, k % LO_SLOTS]), (w_lo[:, k], t_hi[:, k])):
                                for n in range(2):
                                    ins = pe.matmul(ps[4 + 2 * b + n][:, :], w[:, b * P:(b + 1) * P], v[:, n * BANK:(n + 1) * BANK],
                                                    start=False, stop=False, skip_group_check=True)
                        ins.then_inc(tile_used, 1)

            def recurrent():
                norm(2)
                ht_is_ready(2)
                pe.wait_ge(x_stored, 4)
                for i in range(8):
                    n = (2, 3, 0, 1)[i // 2]
                    if i % 2 == 0:
                        pe.wait_ge(win_loaded[n], 16)
                    if i >= 4:
                        pe.wait_ge(rec_copied, i - 3)
                    for j in range(2):
                        for c in range(KC):
                            a = ((i % 2) * 2 + j) * P
                            ins = pe.matmul(ps[4 + i % 4][:, j * SEQ:(j + 1) * SEQ], win[:, n, c, a:a + P], hT[:, c, :],
                                            start=(c == 0), stop=(c == KC - 1))
                    ins.then_inc(rec_psum, 1)
                pe.wait_ge(wax_loaded, 16)
                for i in range(8):
                    h, g = i // 2, i % 2
                    pe.wait_ge(conv_done, 2 * (h + 1))
                    if i >= 4:
                        pe.wait_ge(rg_ready, 2 * (i - 3))
                    for j in range(2):
                        for c in range(2):
                            ins = pe.matmul(ps[i % 4][:, j * SEQ:(j + 1) * SEQ], wax[:, g, h, c, j * P:(j + 1) * P], uc[:, 2 * h + c, :],
                                            start=(c == 0), stop=(c == 1))
                    ins.then_inc(rg_psum, 1)
                pe.wait_ge(y_ready, KC)
                pe.wait_ge(wro_loaded, 16)
                project(wro, 1)

            for _ in range(HI_SLOTS):
                pe.sem_inc(tile_used, 1)
            for _ in range(2):
                pe.sem_inc(gates_psum, 1)
            pe.wait_ge(consts_set, 3)
            norm(0)
            attention()
            peer(0)
            recurrent()
            peer(1)


def kernel(**inputs):
    import numpy as np
    import concourse.bacc as bacc
    from concourse.bass_utils import run_bass_kernel_spmd

    a = {k: np.asarray(v) for k, v in inputs.items()}

    def by_chunk(v):
        return v.reshape(KC, P).T

    windows = np.lib.stride_tricks.sliding_window_view(a["attn_rel_bias"][0][:, ::-1], 2 * P, axis=1)
    u = a["peer_u"].reshape(2, NKEYS, NKEYS, KC, P)
    arrays = {
        "x_in": a["x"].reshape(SEQ, D),
        "norm_g": np.stack([by_chunk(v) for v in (a["attn_norm_g"][0], a["ffn_norm_g"][0], a["rec_norm_g"][0],
                                                  a["ffn_norm_g"][1])], axis=1),
        "w_qkv": a["attn_w_qkv"][0],
        "qk_g": np.stack([np.concatenate([v, v]) for v in (a["attn_q_g"][0], a["attn_k_g"][0])], axis=1),
        "rel_rows": windows[:, P:0:-1].transpose(1, 0, 2),
        "w_out": a["attn_w_out"][0],
        "w_in": a["rec_w_in"][0],
        "rec_p": np.stack([by_chunk(v) for v in (*a["rec_conv_w"][0], a["rec_conv_b"][0], a["rec_b_a"][0],
                                                 a["rec_b_x"][0], a["rec_lambda"][0])], axis=2),
        "w_ax": np.stack([a[n][0].reshape(LRU_HEADS, 2, P, 2 * P).transpose(2, 0, 1, 3) for n in ("rec_w_a", "rec_w_x")], axis=1),
        "rec_w_out": a["rec_w_out"][0],
        "w_q": a["peer_w_q"],
        "keys_t": a["peer_sub_keys"].transpose(3, 0, 1, 2),
        "u_t": u.transpose(0, 2, 4, 3, 1).reshape(2, TILES, P, D),
        "v_t": a["peer_v"].reshape(2, NKEYS, NKEYS, D),
    }
    arrays = {k: np.ascontiguousarray(v) for k, v in arrays.items()}
    nc = bacc.Bacc("TRN2", target_bir_lowering=False, num_devices=1)
    args = {k: nc.dram_tensor(k, v.shape, F32, kind="ExternalInput").ap() for k, v in arrays.items()}
    args["v_t"] = args["v_t"].rearrange("l i j d -> l j i d")
    args["out"] = nc.dram_tensor("out", (SEQ, D), F32, kind="ExternalOutput").ap()
    trunk(nc, **args)
    r = run_bass_kernel_spmd(nc, [arrays], core_ids=[0])
    return r.results[0]["out"].reshape(1, SEQ, D)
```

```python
from contextlib import ExitStack

import concourse.bass as bass
from concourse import mybir

F32 = mybir.dt.float32
F32R = mybir.dt.float32r
BF16 = mybir.dt.bfloat16
U32 = mybir.dt.uint32
ALU = mybir.AluOpType
ACT = mybir.ActivationFunctionType
AX = mybir.AxisListType.X

P = 128
SEQ = 256
D = 1024
TB = SEQ // P
KC = D // P
BANK = 512
EPS = 1e-6

HEADS = 16
HD = D // HEADS
CHUNK = 64
NEG = -1e30

PHEADS = 8
TOPK = 16
NKEYS = 128
RAW_SLOTS = 4
HI_SLOTS = 4
LO_SLOTS = 2
UNROLL = 4
TILES = NKEYS
HALF = TILES // 2
BODIES = HALF // UNROLL
GROUP = 4
GROUPS = SEQ // GROUP
W_SLOTS = 4
HOT_SLOTS = 2
GATE_BANKS = 2
LO_AHEAD = 3
PARTS = 3
EXP_AT = 12
TURN_AT = 14

LRU_HEADS = 4
CONV = 4
LRU_C = 8.0
LOG1P_TERMS = 9

QKV_TILES, PROJ_TILES, UP_TILES = 3 * KC, KC, 2 * KC
AT_QKV = 0
AT_WOUT = AT_QKV + QKV_TILES
AT_WQ = [AT_WOUT + PROJ_TILES, 0]
AT_U = [AT_WQ[0] + UP_TILES, 0]
AT_WIN = AT_U[0] + 2 * TILES
AT_RWOUT = AT_WIN + UP_TILES
AT_WQ[1] = AT_RWOUT + PROJ_TILES
AT_U[1] = AT_WQ[1] + UP_TILES
STREAM = AT_U[1] + 2 * TILES

NORM_BANK = [0, 4, 0, 4]
OUT_BANK = Q_BANK = 0
UP_BANK = 6

ACT_COLS = NKEYS * SEQ
X_SQ, X_DIAG = 30720, 31744
A_BIAS, A_S, A_P, A_PT, A_DIAG = 0, 4096, 6144, 8192, 10240
A_QT, A_KT, A_SQ, A_QKV = 12288, 14336, 16384, 24576
P_QT, P_TOP, P_S, P_KEYS, P_HIT, P_HALF, P_TOPF, P_SLOT = 16384, 17408, 19456, 23552, 23808, 25856, 26368, 26624
R_R, R_A, R_TH, R_WA, R_GATE, R_UPAD, R_UC = 0, 4096, 6144, 8192, 16384, 18432, 20544
UPAD = SEQ + CONV


class Count:

    def __init__(self, sem):
        self.sem, self.n = sem, 0

    def up(self, ins):
        ins.then_inc(self.sem, 1)
        self.n += 1
        return self.n


def trunk(nc, x_in, norm_g, w_qkv, qk_g, rel_rows, w_out, w_in, rec_p, w_ax, rec_w_out, w_q,
          keys_t, u_t, v_t, out):
    ctx = ExitStack()
    with ctx:
        def sb(name, shape, dt=F32):
            return ctx.enter_context(nc.sbuf_tensor(name, shape, dt))

        def sem(name):
            return ctx.enter_context(nc.semaphore(name))

        big = sb("big", [P, ACT_COLS])
        x = sb("x", [P, TB, D])
        h_hi = sb("h_hi", [P, KC, SEQ], F32R)
        h_lo = sb("h_lo", [P, KC, SEQ], F32R)
        raw = sb("raw", [P, RAW_SLOTS, D])
        t_hi = sb("t_hi", [P, HI_SLOTS, D], F32R)
        t_lo = sb("t_lo", [P, LO_SLOTS, D], F32R)
        slotT = sb("slotT", [P, 2, SEQ])
        slot_w = sb("slot_w", [P, SEQ, PARTS], BF16)
        slot_r = sb("slot_r", [P, SEQ])
        hit2 = sb("hit2", [P, GROUP, HALF])
        hot1 = sb("hot1", [P, HOT_SLOTS, GROUP, NKEYS], BF16)
        hot2 = sb("hot2", [P, HOT_SLOTS, GROUP, PARTS, HALF], BF16)
        iota = sb("iota", [P, NKEYS])
        ident = sb("ident", [P, P])
        gains = sb("gains", [P, 4, KC])
        qkg = sb("qkg", [P, 2])
        recp = sb("recp", [P, KC, 8])
        stat = sb("stat", [P, 8])
        qstat = sb("qstat", [P, TB, 32])
        smax = sb("smax", [P, 2, 4])
        ssum = sb("ssum", [P, 2, 4])
        sinv = sb("sinv", [P, 2, 4])
        gsum = sb("gsum", [P, 16])
        sp = sb("sp", [P, 4, KC])
        decay = sb("decay", [P, 2, KC])
        eps = sb("eps", [P, 1])
        ps01 = ctx.enter_context(nc.psum_tensor("ps01", [P, 2 * BANK], F32))
        ps = [ps01[:, 0:BANK], ps01[:, BANK:]] + [ctx.enter_context(nc.psum_tensor(f"ps{i}", [P, BANK], F32)) for i in range(2, 8)]
        gate_iota = ps01[:, 0:NKEYS]
        gate_w = ps01[:, NKEYS:NKEYS + SEQ * PARTS].rearrange("p (t w) -> p t w", w=PARTS)

        def cols(a, n):
            return big[:, a:a + n]

        acts = big[:, :].rearrange("p (j t) -> p j t", t=SEQ)
        x_sq = cols(X_SQ, D)
        x_diag = cols(X_DIAG, TB * P).rearrange("p (b q) -> p b q", b=TB)
        bias = cols(A_BIAS, 4096).rearrange("p (h j) -> p h j", h=HEADS)
        S = cols(A_S, 2048).rearrange("p (s h j) -> p s h j", s=2, h=4)
        Pr = cols(A_P, 2048).rearrange("p (s h j) -> p s h j", s=2, h=4)
        PT = cols(A_PT, 2048).rearrange("p (s b q) -> p s b q", s=2, b=8)
        p_diag = cols(A_DIAG, 1024).rearrange("p (s h q) -> p s h q", s=2, h=4)
        QT = cols(A_QT, 2048).rearrange("p (c t) -> p c t", c=KC)
        KT = cols(A_KT, 2048).rearrange("p (c t) -> p c t", c=KC)
        qkv = cols(A_QKV, 6144).rearrange("p (b m) -> p b m", b=TB)
        qT = cols(P_QT, 1024).rearrange("p (s k t) -> p s k t", s=2, k=2)
        s_sb = cols(P_S, 4096).rearrange("p (h b k n) -> p h b k n", h=PHEADS, b=TB, k=2)
        keys = cols(P_KEYS, 2 * NKEYS).rearrange("p (k n) -> p k n", k=2)
        topv = cols(P_TOP, 512).rearrange("p (b h k j) -> p b h k j", b=TB, h=PHEADS, k=2)
        topi = cols(P_TOP + 512, 512).bitcast(U32).rearrange("p (b h k j) -> p b h k j", b=TB, h=PHEADS, k=2)
        bestv = cols(P_TOP + 1024, 256).rearrange("p (b h j) -> p b h j", b=TB, h=PHEADS)
        besti = cols(P_TOP + 1280, 256).bitcast(U32).rearrange("p (b h j) -> p b h j", b=TB, h=PHEADS)
        cand = cols(P_TOP + 1536, 512).rearrange("p (b c) -> p b c", b=TB)
        hit = cols(P_HIT, 2048).rearrange("p (k j) -> p k j", j=TOPK)
        half_u = cols(P_HALF, 256).bitcast(U32).rearrange("p (k m) -> p k m", k=2)
        half_f = cols(P_HALF + 256, 256).rearrange("p (k m) -> p k m", k=2)
        topf = cols(P_TOPF, 256).rearrange("p (h k j) -> p h k j", h=PHEADS, k=2)
        slot = cols(P_SLOT, 768).rearrange("p (w b m) -> p w b m", w=3, b=TB)
        w_hi = h_hi[:, 0:W_SLOTS, :]
        w_lo = h_lo[:, 0:W_SLOTS, :]
        gate = cols(R_GATE, 2048).rearrange("p (c t) -> p c t", c=KC)
        upad = cols(R_UPAD, KC * UPAD).rearrange("p (c t) -> p c t", c=KC)
        uc = cols(R_UC, 2048).rearrange("p (c t) -> p c t", c=KC)
        wax = cols(R_WA, 4096).rearrange("p (g h c m) -> p g h c m", g=2, h=LRU_HEADS, c=2)
        rg = cols(R_R, 4096).rearrange("p (g c t) -> p g c t", g=2, c=KC)
        ra = cols(R_A, 2048).rearrange("p (c t) -> p c t", c=KC)
        th = cols(R_TH, 2048).rearrange("p (c t) -> p c t", c=KC)

        x_loaded = [sem(f"x_loaded{b}") for b in range(TB)]
        gains_loaded, small_loaded, bias_loaded = sem("gains_loaded"), sem("small_loaded"), sem("bias_loaded")
        keys_loaded, wax_loaded, stored = sem("keys_loaded"), sem("wax_loaded"), sem("stored")
        raw_loaded = [sem(f"raw_loaded{n}") for n in range(RAW_SLOTS)]
        hi_ready, lo_ready, tile_used = sem("tile_hi_ready"), sem("tile_lo_ready"), sem("tile_used")
        consts_set, const_step = sem("consts_set"), sem("const_step")
        ss_ready, rms_ready, diag_ready = sem("ss_ready"), sem("rms_ready"), sem("diag_ready")
        turned, h_hi_ready, h_lo_ready = sem("rows_turned"), sem("h_hi_ready"), sem("h_lo_ready")
        qkv_copied, v1_copied = sem("qkv_copied"), sem("v1_copied")
        qss_ready, qrms_ready, qn_ready = sem("qss_ready"), sem("qrms_ready"), sem("qn_ready")
        qk_psum, q_turned, k_turned = sem("qk_psum"), sem("q_turned"), sem("k_turned")
        masked, sc_psum, sc_ready, sc_max = sem("masked"), sem("sc_psum"), sem("sc_ready"), sem("sc_max")
        probs_ready, pt_psum, pt_ready = sem("probs_ready"), sem("pt_psum"), sem("pt_ready")
        p_diag_ready = sem("p_diag_ready")
        pv_psum, o_hi_ready, o_lo_ready = sem("pv_psum"), sem("o_hi_ready"), sem("o_lo_ready")
        block0_summed, x_added = sem("block0_summed"), sem("x_added")
        q_copied, s_psum, s_copied = sem("q_copied"), sem("s_psum"), sem("s_copied")
        logits_ready, exp_ready, slots_ready = sem("logits_ready"), sem("exp_ready"), sem("slots_ready")
        slot_psum = sem("slot_psum")
        act_ready = sem("act_ready")
        hit2_ready, hot_ready, gates_psum, gated = sem("hit2_ready"), sem("hot_ready"), sem("gates_psum"), sem("gated")
        whi_ready, wlo_ready, x_stored = sem("whi_ready"), sem("wlo_ready"), sem("x_replaced")
        lam_exp, abs_ready = sem("lam_exp"), sem("lam_abs")
        rec_copied, conv_done = sem("rec_copied"), sem("conv_done")
        rg_psum, rg_ready, ra_ready, one_minus, mult_ready, y_ready = map(
            sem, ("rg_psum", "rg_ready", "decay_ready", "variance_ready", "mult_ready", "y_ready"))
        y_hi_ready, y_lo_ready = sem("y_hi_ready"), sem("y_lo_ready")
        dve_step, table_set = sem("dve_step"), sem("table_set")

        block = ctx.enter_context(nc.Block())

        @block.sync
        def _(sp_):
            def tile(n, src):
                sp_.wait_ge(lo_ready, n + 1)
                sp_.dma_start(raw[:, n % RAW_SLOTS, :], src).then_inc(raw_loaded[n % RAW_SLOTS], 16)

            def tiles(n0, table, last, first=0):
                with sp_.Fori(first // UNROLL, last // UNROLL) as g:
                    for k in range(UNROLL):
                        sp_.wait_ge(lo_ready, g * UNROLL + (n0 + k + 1))
                        sp_.dma_start(raw[:, k, :], table[g * UNROLL + k]).then_inc(raw_loaded[k], 16)

            def qkv_tile(i):
                return w_qkv.rearrange("(c p) (m d) -> m c p d", p=P, d=D)[i // KC, i % KC]

            for b in range(TB):
                sp_.dma_start(x[:, b, :], x_in[b * P:(b + 1) * P, :]).then_inc(x_loaded[b], 16)
            sp_.dma_start(gains[:, :, :], norm_g).then_inc(gains_loaded, 16)
            for i in range(RAW_SLOTS):
                tile(AT_QKV + i, qkv_tile(i))
            for dst, src in ((qkg[:, :], qk_g), (recp[:, :, :], rec_p)):
                sp_.dma_start(dst, src).then_inc(small_loaded, 16)
            for a, b, n in ((0, CHUNK, 3 * CHUNK), (CHUNK, P, 4 * CHUNK)):
                sp_.dma_start(bias[a:b, :, 0:n], rel_rows[a:b, :, 0:n]).then_inc(bias_loaded, 16)
            sp_.dma_start(keys, keys_t[0]).then_inc(keys_loaded, 16)
            for i in range(RAW_SLOTS, QKV_TILES):
                tile(AT_QKV + i, qkv_tile(i))
            tiles(AT_WOUT, w_out.rearrange("(c p) d -> c p d", p=P), PROJ_TILES)
            for l in range(2):
                tiles(AT_WQ[l], w_q[l], UP_TILES)
                tiles(AT_U[l], u_t[l], TILES)
                if l == 0:
                    tiles(AT_U[l] + TILES, v_t[l], HALF + 4 * UNROLL)
                    sp_.wait_ge(wlo_ready, HALF)
                    sp_.dma_start(wax, w_ax).then_inc(wax_loaded, 16)
                    tiles(AT_U[l] + TILES, v_t[l], TILES, HALF + 4 * UNROLL)
                    tiles(AT_WIN, w_in, UP_TILES)
                    sp_.wait_ge(wlo_ready, TILES)
                    sp_.dma_start(keys, keys_t[1]).then_inc(keys_loaded, 16)
                    tiles(AT_RWOUT, rec_w_out.rearrange("(c p) d -> c p d", p=P), PROJ_TILES)
                else:
                    tiles(AT_U[l] + TILES, v_t[l], TILES)
            for i in range(2 * TB):
                b, half_row = i // 2, slice(i % 2 * BANK, (i % 2 + 1) * BANK)
                sp_.wait_ge(x_stored, 4 + i + 1)
                sp_.dma_start(out[b * P:(b + 1) * P, half_row], x[:, b, half_row]).then_inc(stored, 16)
            sp_.wait_ge(stored, 64)

        @block.gpsimd
        def _(pool):
            pool.iota(iota[:, :], pattern=[[1, NKEYS]], base=0, channel_multiplier=0,
                      allow_small_or_imprecise_dtypes=True).then_inc(consts_set, 1)
            pool.memset(ident[:, :], 0.0).then_inc(const_step, 1)
            pool.wait_ge(const_step, 1)
            pool.affine_select(out=ident[:, :], in_=ident[:, :], compare_op=ALU.not_equal, fill=1.0, base=0,
                               pattern=[[-1, P]], channel_multiplier=1).then_inc(consts_set, 1)
            for _ in range(RAW_SLOTS):
                pool.sem_inc(lo_ready, 1)

            with pool.Fori(0, STREAM // UNROLL) as g:
                for k in range(UNROLL):
                    pool.wait_ge(tile_used, g * UNROLL + (k + 1 + HI_SLOTS - LO_SLOTS))
                    pool.wait_ge(hi_ready, g * UNROLL + (k + 1))
                    pool.tensor_tensor(t_lo[:, k % LO_SLOTS, :], raw[:, k, :], t_hi[:, k, :].bitcast(F32),
                                       ALU.subtract).then_inc(lo_ready, 1)

        @block.scalar
        def _(act):
            def hi_part(n):
                act.wait_ge(tile_used, n + 1)
                act.wait_ge(raw_loaded[n % RAW_SLOTS], 16 * (n // RAW_SLOTS + 1))
                act.activation(t_hi[:, n % HI_SLOTS, :], raw[:, n % RAW_SLOTS, :], ACT.Copy).then_inc(hi_ready, 1)

            def next_hi(g, k, n0):
                act.wait_ge(tile_used, g * UNROLL + (n0 + k + 1 + HI_SLOTS))
                act.wait_ge(raw_loaded[k], g * 16 + 16 * (n0 // UNROLL + 2))
                act.activation(t_hi[:, k, :], raw[:, k, :], ACT.Copy).then_inc(hi_ready, 1)

            tables = Count(table_set)

            def want_table(func):
                if tables.n:
                    act.wait_ge(table_set, tables.n)
                tables.up(act.activation(stat[:, 6:7], eps[:, :], func))

            def norm(n, x_block, next_tiles=()):
                want_table(ACT.Sqrt)
                for b in range(TB):
                    act.wait_ge(*x_block(b))
                    if b >= 1:
                        act.wait_ge(ss_ready, TB * n + b)
                    act.activation(x_sq, x[:, b, :], ACT.Square, accum_out=stat[:, b:b + 1]).then_inc(ss_ready, 1)
                    act.wait_ge(ss_ready, TB * n + b + 1)
                    act.activation(stat[:, 2 + b:3 + b], stat[:, b:b + 1], ACT.Sqrt, bias=eps[:, :],
                                   scale=1.0 / D).then_inc(rms_ready, 1)
                for t in next_tiles[:1]:
                    hi_part(t)
                if n == 0:
                    act.wait_ge(gains_loaded, 16)
                for c in range(KC):
                    act.wait_ge(turned, 4 * n + c % 4 + 1)
                    if c >= 4:
                        act.wait_ge(h_lo_ready, KC * n + c - 3)
                    src = ps[NORM_BANK[n] + c % 4][:, (c // 4) * SEQ:(c // 4 + 1) * SEQ]
                    act.activation(h_hi[:, c, :], src, ACT.Copy, scale=gains[:, n, c:c + 1]).then_inc(h_hi_ready, 1)
                for t in next_tiles[1:]:
                    hi_part(t)

            def attention():
                act.wait_ge(small_loaded, 32)
                act.activation(sp[:, 0, :], recp[:, :, 7], ACT.Abs).then_inc(abs_ready, 1)
                act.wait_ge(abs_ready, 1)
                act.activation(sp[:, 1, :], sp[:, 0, :], ACT.Exp, scale=-1.0).then_inc(lam_exp, 1)

                def head_rms(m):
                    for b in range(TB):
                        act.wait_ge(qss_ready, TB * m + b + 1)
                        act.activation(qstat[:, b, m * HEADS:(m + 1) * HEADS], qstat[:, b, m * HEADS:(m + 1) * HEADS],
                                       ACT.Sqrt, bias=eps[:, :], scale=1.0 / HD).then_inc(qrms_ready, 1)

                def copy_projection(m, banks=4):
                    act.wait_ge(tile_used, AT_QKV + (m + 1) * KC + HI_SLOTS)
                    for i in range(banks):
                        b, n = i // 2, i % 2
                        act.activation(qkv[:, b, m * D + n * BANK:m * D + (n + 1) * BANK], ps[4 * ((m + 1) % 2) + i][:, :],
                                       ACT.Copy).then_inc(qkv_copied, 1)

                def probs(s):
                    g, b = s // TB, s % TB
                    w = (b + 1) * P
                    act.wait_ge(sc_max, s + 1)
                    if s >= 2:
                        act.wait_ge(pt_psum, s - 1)
                    for h in range(4):
                        act.activation(Pr[:, s % 2, h, 0:w], S[:, s % 2, h, 0:w], ACT.Exp,
                                       bias=smax[:, s % 2, h:h + 1], accum_out=ssum[:, s % 2, h:h + 1]).then_inc(probs_ready, 1)

                def copy_turned(s):
                    act.wait_ge(pt_psum, s + 1)
                    if s >= 2:
                        act.wait_ge(pv_psum, s - 1)
                    for m in range(s % TB + 1):
                        act.activation(PT[:, s % 2, 4 * m:4 * m + 4, :], ps[4 + m][:, :].rearrange("p (b q) -> p b q", b=4),
                                       ACT.Copy).then_inc(pt_ready, 1)

                def outputs(s):
                    g, b = s // TB, s % TB
                    act.wait_ge(pv_psum, s + 1)
                    for r in range(2):
                        rows = slice(r * HD, (r + 1) * HD)
                        act.activation(h_hi[rows, 2 * g:2 * g + 2, b * P:(b + 1) * P],
                                       ps[6 + s % 2][rows, :].rearrange("p (m r q) -> p m r q", m=2, r=2)[:, :, r, :],
                                       ACT.Copy).then_inc(o_hi_ready, 1)

                for m in range(2):
                    for c in range(KC):
                        hi_part(AT_QKV + m * KC + c + HI_SLOTS)
                    copy_projection(m)
                    head_rms(m)
                for c in range(4):
                    hi_part(AT_QKV + 2 * KC + c + HI_SLOTS)
                for b in range(TB):
                    for m in range(2):
                        i = b * 4 + 2 + m
                        act.wait_ge(qk_psum, i + 1)
                        act.activation(KT[:, 4 * m:4 * m + 4, b * P:(b + 1) * P],
                                       ps[i % 4][:, :].rearrange("p (c t) -> p c t", c=4), ACT.Copy,
                                       scale=qkg[:, 1:2]).then_inc(k_turned, 1)
                    hi_part(AT_QKV + 2 * KC + 4 + b + HI_SLOTS)
                probs(0)
                hi_part(AT_QKV + 2 * KC + 6 + HI_SLOTS)
                copy_projection(2, 2)
                for s in range(8):
                    if s < 7:
                        probs(s + 1)
                    copy_turned(s)
                    if s == 0:
                        hi_part(AT_QKV + 2 * KC + 7 + HI_SLOTS)
                    if s >= 1:
                        outputs(s - 1)
                outputs(7)
                for c in range(PROJ_TILES - LO_SLOTS):
                    hi_part(AT_WOUT + c + HI_SLOTS)

            def peer(l):
                n = 2 * l + 1
                norm(n, lambda b: (x_added, 4 * l + 2 * (b + 1)),
                     [(AT_WOUT, AT_RWOUT)[l] + HI_SLOTS + c for c in range(PROJ_TILES - LO_SLOTS, PROJ_TILES)])
                for h in range(PHEADS):
                    for i in (2 * h, 2 * h + 1):
                        hi_part(AT_WQ[l] + i + HI_SLOTS)
                    act.wait_ge(tile_used, AT_WQ[l] + 2 * (h + 1) + HI_SLOTS)
                    if h >= 2:
                        act.wait_ge(s_psum, l * PHEADS + h - 1)
                    act.activation(qT[:, h % 2], ps[Q_BANK + h % 2][:, :].rearrange("p (k t) -> p k t", k=2), ACT.Copy).then_inc(q_copied, 1)
                    if h >= 1:
                        key_scores(l, h - 1)
                key_scores(l, PHEADS - 1)

                def gelu(g, k, half):
                    n0 = AT_U[l] + half * HALF
                    act.wait_ge(tile_used, g * UNROLL + (n0 + k + 1 + HI_SLOTS))
                    act.activation(big[:, bass.ds((g * UNROLL + half * HALF + k - 1) * SEQ, 2 * SEQ)], ps[UP_BANK + k // 2][:, :],
                                   ACT.Gelu_apprx_tanh).then_inc(act_ready, 1)

                def up(half, a, b):
                    with act.Fori(a, b) as g:
                        for k in range(UNROLL):
                            next_hi(g, k, AT_U[l] + half * HALF)
                            if k % 2:
                                gelu(g, k, half)

                want_table(ACT.Gelu_apprx_tanh)
                up(0, 0, EXP_AT)
                act.wait_ge(logits_ready, l + 1)
                act.activation(slot[:, 2], slot[:, 2], ACT.Exp).then_inc(exp_ready, 1)
                want_table(ACT.Gelu_apprx_tanh)
                up(0, EXP_AT, BODIES)
                act.wait_ge(slot_psum, l + 1)
                up(1, 0, BODIES - 1)
                for k in range(UNROLL - 1):
                    next_hi(BODIES - 1, k, AT_U[l] + HALF)
                    if k == 1:
                        gelu(BODIES - 1, k, 1)

                def gated_hi(at, k, count):
                    act.wait_ge(tile_used, count + (AT_U[l] + TILES - l * TILES + 1))
                    act.activation(w_hi[:, k, :], acts[:, at, :], ACT.Copy).then_inc(whi_ready, 1)

                for half in range(2):
                    def after_half(k):
                        hi_part(AT_U[l] + TILES + half * HALF + k)

                    if half == 0:
                        act.wait_ge(tile_used, AT_U[l] + TILES + HI_SLOTS)
                    else:
                        for k in range(UNROLL - 1):
                            after_half(k)
                    act.wait_ge(gated, l * 2 * GROUPS + (half + 1) * GROUPS + GATE_BANKS)
                    for k in range(UNROLL):
                        if half == 1 and k == UNROLL - 1:
                            after_half(k)
                        gated_hi(half * HALF + k, k, l * TILES + half * HALF + k)
                        if half == 0 and k == 0:
                            gelu(BODIES - 1, UNROLL - 1, 1)
                    if half == 0:
                        next_hi(BODIES - 1, UNROLL - 1, AT_U[l] + HALF)
                    with act.Fori(0, BODIES - 1) as g:
                        for k in range(UNROLL):
                            gated_hi(g * UNROLL + (half * HALF + UNROLL + k), k, g * UNROLL + (l * TILES + half * HALF + UNROLL + k))
                            next_hi(g, k, AT_U[l] + TILES + half * HALF)
                if l == 0:
                    for k in range(UNROLL - LO_SLOTS):
                        hi_part(AT_WIN + k)

            def key_scores(l, h):
                act.wait_ge(s_psum, l * PHEADS + h + 1)
                act.activation(s_sb[:, h].rearrange("p b k n -> p (b k n)"), ps[Q_BANK + 2 + h % 2][:, :], ACT.Copy).then_inc(s_copied, 1)

            def recurrent():
                norm(2, lambda b: (x_stored, 2 * (b + 1)),
                     [AT_WIN + k for k in range(UNROLL - LO_SLOTS, UNROLL)])

                def next_tile(j):
                    hi_part(AT_WIN + j + HI_SLOTS)

                def sigmoids(h):
                    for g in range(2):
                        act.wait_ge(rg_psum, 2 * h + g + 1)
                        for c in range(2):
                            act.activation(rg[:, g, 2 * h + c, :], ps[(2 * h + g) % 4][:, c * SEQ:(c + 1) * SEQ], ACT.Sigmoid,
                                           bias=recp[:, 2 * h + c, 5 + g:6 + g]).then_inc(rg_ready, 1)

                def decays(e):
                    act.wait_ge(rg_ready, 8 * (e + 1))
                    for c in range(4 * e, 4 * e + 4):
                        act.activation(th[:, c, :], rg[:, 0, c, :], ACT.Tanh, scale=decay[:, 1, c:c + 1])
                        act.activation(ra[:, c, :], rg[:, 0, c, :], ACT.Exp, scale=decay[:, 0, c:c + 1]).then_inc(ra_ready, 1)

                def mult(e):
                    act.wait_ge(one_minus, e + 1)
                    act.activation(th[:, 4 * e:4 * e + 4, :], th[:, 4 * e:4 * e + 4, :], ACT.Sqrt).then_inc(mult_ready, 1)

                def gelu_gate(i):
                    act.wait_ge(tile_used, AT_WIN + KC + 2 * (i + 1) + HI_SLOTS)
                    act.activation(gate[:, 2 * i:2 * i + 2, :], ps[4 + i][:, :].rearrange("p (c t) -> p c t", c=2),
                                   ACT.Gelu_apprx_tanh).then_inc(rec_copied, 1)

                def y_hi_part(c):
                    act.wait_ge(y_ready, c + 1)
                    act.activation(h_hi[:, c, :], rg[:, 0, c, :], ACT.Copy).then_inc(y_hi_ready, 1)

                for i in range(4):
                    next_tile(2 * i)
                    next_tile(2 * i + 1)
                    act.wait_ge(tile_used, AT_WIN + 2 * (i + 1) + HI_SLOTS)
                    act.activation(upad[:, 2 * i:2 * i + 2, CONV - 1:CONV - 1 + SEQ],
                                   ps[4 + i][:, :].rearrange("p (c t) -> p c t", c=2), ACT.Copy).then_inc(rec_copied, 1)
                    if i == 2:
                        want_table(ACT.Sigmoid)
                        sigmoids(0)
                for h in range(1, LRU_HEADS):
                    sigmoids(h)
                decays(0)
                next_tile(KC)
                decays(1)
                next_tile(KC + 1)
                mult(0)
                next_tile(KC + 2)
                next_tile(KC + 3)
                mult(1)
                gelu_gate(0)
                gelu_gate(1)
                next_tile(KC + 4)
                next_tile(KC + 5)
                gelu_gate(2)
                next_tile(KC + 6)
                act.wait_ge(tile_used, AT_WIN + UP_TILES + HI_SLOTS)
                y_hi_part(0)
                y_hi_part(1)
                gelu_gate(3)
                for c in range(2, 6):
                    y_hi_part(c)
                next_tile(KC + 7)
                for c in range(6, KC):
                    y_hi_part(c)
                for c in range(PROJ_TILES - LO_SLOTS):
                    hi_part(AT_RWOUT + c + HI_SLOTS)

            for _ in range(2):
                act.sem_inc(act_ready, 1)
            act.wait_ge(consts_set, 3)
            norm(0, lambda b: (x_loaded[b], 16), [AT_QKV + i for i in range(HI_SLOTS)])
            attention()
            peer(0)
            recurrent()
            peer(1)

        @block.vector
        def _(dve):
            step = Count(dve_step)

            def link(ins):
                dve.wait_ge(step.sem, step.up(ins))

            def norm(n, add_block=lambda b: None):
                for b in range(TB):
                    add_block(b)
                    dve.wait_ge(rms_ready, TB * n + b + 1)
                    link(dve.reciprocal(stat[:, 4 + b:5 + b], stat[:, 2 + b:3 + b]))
                    dve.tensor_scalar(x_diag[:, b, :], ident[:, :], stat[:, 4 + b:5 + b], None, ALU.mult).then_inc(diag_ready, 1)
                if n == 0:
                    dve.wait_ge(gains_loaded, 16)
                for c in range(KC):
                    dve.wait_ge(h_hi_ready, KC * n + c + 1)
                    src = ps[NORM_BANK[n] + c % 4][:, (c // 4) * SEQ:(c // 4 + 1) * SEQ]
                    dve.scalar_tensor_tensor(out=h_lo[:, c, :], in0=src, scalar=gains[:, n, c:c + 1], in1=h_hi[:, c, :].bitcast(F32),
                                             op0=ALU.mult, op1=ALU.subtract).then_inc(h_lo_ready, 1)

            def block_summed(count, n):
                return lambda b: dve.wait_ge(block0_summed, count) if b == 0 else dve.wait_ge(tile_used, n + HI_SLOTS)

            def add_projection(m):
                wait_block = block_summed(2 * m + 1, (AT_WOUT, AT_RWOUT)[m] + PROJ_TILES)

                def add(b):
                    wait_block(b)
                    for n in range(2):
                        xs = x[:, b, n * BANK:(n + 1) * BANK]
                        dve.tensor_tensor(xs, xs, ps[OUT_BANK + 2 * b + n][:, :], ALU.add).then_inc(x_added, 1)
                return add

            def add_experts(l):
                wait_block = block_summed(2 * l + 2, AT_U[l] + 2 * TILES)

                def add(b):
                    wait_block(b)
                    for n in range(2):
                        xs = x[:, b, n * BANK:(n + 1) * BANK]
                        dve.tensor_tensor(xs, xs, ps[4 + 2 * b + n][:, :], ALU.add).then_inc(x_stored, 1)
                return add

            def attention():
                softplus()
                dve.memset(bias[0:CHUNK, :, 3 * CHUNK:4 * CHUNK], NEG).then_inc(masked, 1)
                sq = cols(A_SQ, D)
                for m in range(2):
                    for b in range(TB):
                        dve.wait_ge(qkv_copied, 4 * m + 2 * (b + 1))
                        part = qkv[:, b, m * D:(m + 1) * D]
                        link(dve.tensor_tensor(sq, part, part, ALU.mult))
                        dve.tensor_reduce(qstat[:, b, m * HEADS:(m + 1) * HEADS], sq.rearrange("p (h d) -> p h d", d=HD), AX,
                                          ALU.add).then_inc(qss_ready, 1)
                        dve.wait_ge(qss_ready, TB * m + b + 1)
                    for b in range(TB):
                        dve.wait_ge(qrms_ready, TB * m + b + 1)
                        stats = qstat[:, b, m * HEADS:(m + 1) * HEADS]
                        link(dve.reciprocal(stats, stats))
                        part = qkv[:, b, m * D:(m + 1) * D].rearrange("p (h d) -> p h d", d=HD)
                        dve.tensor_tensor(part, part, stats.unsqueeze(2).to_broadcast([P, HEADS, HD]), ALU.mult).then_inc(qn_ready, 1)
                for b in range(TB):
                    for m in range(2):
                        i = b * 4 + m
                        dve.wait_ge(qk_psum, i + 1)
                        dve.tensor_scalar(QT[:, 4 * m:4 * m + 4, b * P:(b + 1) * P],
                                          ps[i % 4][:, :].rearrange("p (c t) -> p c t", c=4), qkg[:, 0:1], None,
                                          ALU.mult).then_inc(q_turned, 1)
                dve.wait_ge(bias_loaded, 32)
                dve.wait_ge(masked, 1)

                def scores(s):
                    g, b = s // TB, s % TB
                    w = (b + 1) * P
                    dve.wait_ge(sc_psum, s + 1)
                    if s >= 2:
                        dve.wait_ge(probs_ready, 4 * (s - 1))
                    for r in range(2):
                        dve.scalar_tensor_tensor(
                            out=S[:, s % 2, r:4:2, 0:w], in0=ps[2 * (s % 2) + r][:, :].rearrange("p (m j) -> p m j", m=2)[:, :, 0:w],
                            scalar=HD ** -0.5, in1=bias[:, 4 * g + r:4 * g + 4:2, 2 * P - w:2 * P], op0=ALU.mult,
                            op1=ALU.add).then_inc(sc_ready, 1)
                    dve.wait_ge(sc_ready, 2 * (s + 1))
                    dve.tensor_reduce(smax[:, s % 2, :], S[:, s % 2, :, 0:w], AX, ALU.max, negate=True).then_inc(sc_max, 1)

                def diagonals(s):
                    dve.wait_ge(probs_ready, 4 * (s + 1))
                    if s >= 2:
                        dve.wait_ge(p_diag_ready, s - 1)
                    link(dve.reciprocal(sinv[:, s % 2, :], ssum[:, s % 2, :]))
                    if s >= 2:
                        dve.wait_ge(pt_psum, s - 1)
                    shape = [P, 4, P]
                    dve.tensor_tensor(p_diag[:, s % 2], ident[:, :].unsqueeze(1).to_broadcast(shape),
                                      sinv[:, s % 2, :].unsqueeze(2).to_broadcast(shape), ALU.mult).then_inc(p_diag_ready, 1)

                def outputs(s):
                    g, b = s // TB, s % TB
                    for r in range(2):
                        rows = slice(r * HD, (r + 1) * HD)
                        part = (rows, slice(2 * g, 2 * g + 2), slice(b * P, (b + 1) * P))
                        dve.wait_ge(o_hi_ready, 2 * s + 2)
                        dve.tensor_tensor(h_lo[part], ps[6 + s % 2][rows, :].rearrange("p (m r q) -> p m r q", m=2, r=2)[:, :, r, :],
                                          h_hi[part].bitcast(F32), ALU.subtract).then_inc(o_lo_ready, 1)

                scores(0)
                diagonals(0)
                scores(1)
                dve.wait_ge(tile_used, AT_QKV + QKV_TILES + HI_SLOTS)
                for n in range(2):
                    a = 2 * D + n * BANK
                    dve.tensor_copy(qkv[:, 1, a:a + BANK], ps[6 + n][:, :]).then_inc(v1_copied, 1)
                for s in range(8):
                    if s < 6:
                        scores(s + 2)
                    if s < 7:
                        diagonals(s + 1)
                    if s >= 1:
                        outputs(s - 1)
                outputs(7)

            def top16(values, index, source):
                for r in range(2):
                    half = slice(8 * r, 8 * r + 8)
                    for v, s in zip(values, source):
                        n = step.up(dve.max(v[:, half], s))
                    dve.wait_ge(step.sem, n)
                    for v, i, s in zip(values, index, source):
                        n = step.up(dve.max_index(i[:, half], v[:, half], s))
                    if r == 0:
                        dve.wait_ge(step.sem, n)
                        for v, s in zip(values, source):
                            n = step.up(dve.match_replace(s, v[:, half], s, -3e38))
                        dve.wait_ge(step.sem, n)

            def peer(l):
                norm(2 * l + 1, add_projection(l))
                for h in range(PHEADS):
                    dve.wait_ge(s_copied, l * PHEADS + h + 1)
                    pairs = [(b, k) for b in range(TB) for k in range(2)]
                    top16([topv[:, b, h, k, :] for b, k in pairs], [topi[:, b, h, k, :] for b, k in pairs],
                          [s_sb[:, h, b, k, :] for b, k in pairs])
                    dve.wait_ge(step.sem, step.n)
                    for b in range(TB):
                        m = step.up(dve.tensor_tensor(
                            cand[:, b, :].rearrange("p (i j) -> p i j", i=TOPK),
                            topv[:, b, h, 0, :].unsqueeze(2).to_broadcast([P, TOPK, TOPK]),
                            topv[:, b, h, 1, :].unsqueeze(1).to_broadcast([P, TOPK, TOPK]), ALU.add))
                    dve.wait_ge(step.sem, m)
                    top16([bestv[:, b, h, :] for b in range(TB)], [besti[:, b, h, :] for b in range(TB)],
                          [cand[:, b, :] for b in range(TB)])
                    dve.wait_ge(step.sem, step.n)
                for b in range(TB):
                    flat = besti[:, b].rearrange("p h j -> p (h j)")
                    dve.tensor_single_scalar(half_u[:, 0, :], flat, 4, ALU.logical_shift_right)
                    link(dve.tensor_single_scalar(half_u[:, 1, :], flat, TOPK - 1, ALU.bitwise_and))
                    dve.tensor_copy(half_f, half_u)
                    link(dve.tensor_copy(topf, topi[:, b]))
                    hit4 = hit.rearrange("p (h k) j -> p h k j", h=PHEADS)
                    for k in range(2):
                        link(dve.tensor_tensor(hit, half_f[:, k, :].unsqueeze(2).to_broadcast([P, PHEADS * TOPK, TOPK]),
                                               iota[:, 0:TOPK].unsqueeze(1).to_broadcast([P, PHEADS * TOPK, TOPK]), ALU.is_equal))
                        link(dve.tensor_tensor(hit4, hit4, topf[:, :, k, :].unsqueeze(2).to_broadcast([P, PHEADS, TOPK, TOPK]), ALU.mult))
                        link(dve.tensor_reduce(slot[:, k, b, :], hit, AX, ALU.add))
                    ins = dve.tensor_tensor(slot[:, 2, b, :].rearrange("p (h j) -> p h j", h=PHEADS), bestv[:, b],
                                            bestv[:, b, :, 0:1].to_broadcast([P, PHEADS, TOPK]), ALU.subtract)
                    if b == 0:
                        link(ins)
                ins.then_inc(logits_ready, 1)
                dve.wait_ge(exp_ready, l + 1)
                w3 = slot[:, 2].rearrange("p b (h j) -> p (b h) j", h=PHEADS)
                link(dve.tensor_reduce(gsum[:, :], w3, AX, ALU.add))
                link(dve.reciprocal(gsum[:, :], gsum[:, :]))
                dve.tensor_tensor(w3, w3, gsum[:, :].unsqueeze(2).to_broadcast([P, TB * PHEADS, TOPK]), ALU.mult).then_inc(slots_ready, 1)
                dve.wait_ge(slot_psum, l + 1)
                dve.tensor_copy(slotT[:, :, :].rearrange("p w t -> p (w t)"), ps[2][:, :])
                left = ps[3][:, 0:SEQ]
                for part in range(PARTS):
                    link(dve.tensor_copy(slot_w[:, :, part], left))
                    if part < PARTS - 1:
                        link(dve.tensor_tensor(slot_r[:, :], left, slot_w[:, :, part], ALU.subtract))
                        left = slot_r[:, :]
                dve.tensor_copy(gate_iota, iota[:, :])
                link(dve.tensor_copy(gate_w, slot_w[:, :, :]))

                def hot(g, k, half):
                    n = g * UNROLL + ((l * 2 + half) * GROUPS + k + 1)
                    at = bass.ds(g * (UNROLL * GROUP) + k * GROUP, GROUP)

                    def one_hot(out_, width, row):
                        shape = [P, GROUP, width]
                        return dve.tensor_tensor(out_, gate_iota[:, 0:width].unsqueeze(1).to_broadcast(shape),
                                                 slotT[:, row, at].unsqueeze(2).to_broadcast(shape), ALU.is_equal)

                    if not (isinstance(n, int) and n == 1):
                        dve.wait_ge(hot_ready, n - 1)
                    one_hot(hit2[:, :, :], HALF, 1).then_inc(hit2_ready, 1)
                    dve.wait_ge(gates_psum, n)
                    one_hot(hot1[:, k % 2], NKEYS, 0)
                    dve.wait_ge(hit2_ready, n)
                    shape = [P, GROUP, PARTS, HALF]
                    dve.tensor_tensor(hot2[:, k % 2], hit2[:, :, :].unsqueeze(2).to_broadcast(shape),
                                      gate_w[:, at, :].unsqueeze(3).to_broadcast(shape), ALU.mult).then_inc(hot_ready, 1)

                def apply(g, k, half):
                    dve.wait_ge(gates_psum, g * UNROLL + ((l * 2 + half) * GROUPS + k + 1 + GATE_BANKS))
                    a = acts[:, half * HALF:(half + 1) * HALF, bass.ds(g * (UNROLL * GROUP) + k * GROUP, GROUP)]
                    dve.tensor_tensor(a, a, ps[2 + k % 2][:, 0:GROUP * HALF].rearrange("p (t j) -> p j t", t=GROUP),
                                      ALU.mult).then_inc(gated, 1)

                def gated_lo(at, k, count):
                    dve.wait_ge(whi_ready, count + 1)
                    dve.tensor_tensor(w_lo[:, k, :], acts[:, at, :], w_hi[:, k, :].bitcast(F32), ALU.subtract).then_inc(wlo_ready, 1)

                for k in range(HOT_SLOTS):
                    hot(0, k, 0)
                dve.wait_ge(act_ready, l * TILES // 2 + HALF // 2 + 2)
                with dve.Fori(0, BODIES - 1) as g:
                    for k in range(UNROLL):
                        apply(g, k, 0)
                        hot(g, k + HOT_SLOTS, 0)
                for k in range(UNROLL):
                    apply(BODIES - 1, k, 0)
                    if k < UNROLL - HOT_SLOTS:
                        hot(BODIES - 1, k + HOT_SLOTS, 0)
                link(dve.tensor_scalar(slotT[:, 1, :], slotT[:, 1, :], -float(HALF), None, ALU.add))
                hot(0, 0, 1)
                for k in range(LO_AHEAD):
                    gated_lo(k, k, l * TILES + k)
                for k in range(1, HOT_SLOTS):
                    hot(0, k, 1)
                dve.wait_ge(act_ready, (l + 1) * TILES // 2 + 2)
                with dve.Fori(0, BODIES - 1) as g:
                    for k in range(UNROLL):
                        apply(g, k, 1)
                        hot(g, k + HOT_SLOTS, 1)
                        gated_lo(g * UNROLL + (LO_AHEAD + k), (LO_AHEAD + k) % W_SLOTS, g * UNROLL + (l * TILES + LO_AHEAD + k))
                for k in range(UNROLL):
                    apply(BODIES - 1, k, 1)
                    if k < UNROLL - HOT_SLOTS:
                        hot(BODIES - 1, k + HOT_SLOTS, 1)
                    if k < UNROLL - LO_AHEAD:
                        n = HALF - UNROLL + LO_AHEAD + k
                        gated_lo(n, n % W_SLOTS, l * TILES + n)
                with dve.Fori(0, BODIES) as g:
                    for k in range(UNROLL):
                        gated_lo(g * UNROLL + (HALF + k), k, g * UNROLL + (l * TILES + HALF + k))

            def softplus():
                lam = recp[:, :, 7]
                dve.wait_ge(small_loaded, 32)
                dve.wait_ge(lam_exp, 1)
                e, z, z2, acc = (sp[:, i, :] for i in (1, 2, 3, 0))
                link(dve.tensor_scalar(z, e, 2.0, None, ALU.add))
                link(dve.reciprocal(z, z))
                link(dve.tensor_tensor(z, z, e, ALU.mult))
                link(dve.tensor_tensor(z2, z, z, ALU.mult))
                link(dve.memset(acc, 1.0 / (2 * LOG1P_TERMS + 1)))
                for n in range(LOG1P_TERMS - 1, -1, -1):
                    link(dve.tensor_tensor(acc, acc, z2, ALU.mult))
                    link(dve.tensor_scalar(acc, acc, 1.0 / (2 * n + 1), None, ALU.add))
                link(dve.tensor_tensor(acc, acc, z, ALU.mult))
                link(dve.tensor_scalar(e, lam, -1.0, 0.0, ALU.mult, ALU.max))
                link(dve.scalar_tensor_tensor(out=z, in0=acc, scalar=2.0, in1=e, op0=ALU.mult, op1=ALU.add))
                dve.tensor_scalar(decay[:, 0, :], z, -LRU_C, None, ALU.mult)
                link(dve.tensor_scalar(decay[:, 1, :], z, LRU_C, None, ALU.mult))

            def recurrent():
                norm(2, add_experts(0))
                dve.memset(upad[:, :, 0:CONV - 1], 0.0).then_inc(dve_step, 1)
                step.n += 1
                dve.wait_ge(dve_step, step.n)
                for i in range(4):
                    dve.wait_ge(rec_copied, i + 1)
                    for k in range(CONV):
                        for c in (2 * i, 2 * i + 1):
                            src = upad[:, c, k:k + SEQ]
                            if k == 0:
                                ins = dve.tensor_scalar(uc[:, c, :], src, recp[:, c, 0:1], recp[:, c, 4:5], ALU.mult, ALU.add)
                            else:
                                ins = dve.scalar_tensor_tensor(out=uc[:, c, :], in0=src, scalar=recp[:, c, k:k + 1], in1=uc[:, c, :],
                                                               op0=ALU.mult, op1=ALU.add)
                            if k == CONV - 1:
                                ins.then_inc(conv_done, 1)
                            elif c % 2:
                                link(ins)
                dve.wait_ge(conv_done, 8)
                for e in range(2):
                    dve.wait_ge(rg_ready, 8 * (e + 1))
                    half = slice(4 * e, 4 * e + 4)
                    link(dve.tensor_tensor(rg[:, 1, half, :], rg[:, 1, half, :], uc[:, half, :], ALU.mult))
                for e in range(2):
                    dve.wait_ge(ra_ready, 4 * (e + 1))
                    half = slice(4 * e, 4 * e + 4)
                    link(dve.tensor_tensor(rg[:, 0, half, :], ra[:, half, :], ra[:, half, :], ALU.mult))
                    dve.scalar_tensor_tensor(out=th[:, half, :], in0=rg[:, 0, half, :], scalar=1.0, in1=th[:, half, :],
                                             op0=ALU.add, op1=ALU.mult).then_inc(one_minus, 1)

                def scans(e):
                    half = slice(4 * e, 4 * e + 4)
                    dve.wait_ge(mult_ready, e + 1)
                    link(dve.tensor_tensor(rg[:, 1, half, :], rg[:, 1, half, :], th[:, half, :], ALU.mult))
                    for c in range(4 * e, 4 * e + 4):
                        ins = dve.tensor_tensor_scan(uc[:, c, :], ra[:, c, :], rg[:, 1, c, :], 0.0, ALU.mult, ALU.add)
                    link(ins)

                def gated_outputs(first, last):
                    for c in range(first, last):
                        dve.wait_ge(rec_copied, 4 + c // 2 + 1)
                        dve.tensor_tensor(rg[:, 0, c, :], uc[:, c, :], gate[:, c, :], ALU.mult).then_inc(y_ready, 1)

                def y_lo_part(first, last):
                    for c in range(first, last):
                        dve.wait_ge(y_hi_ready, c + 1)
                        dve.tensor_tensor(h_lo[:, c, :], rg[:, 0, c, :], h_hi[:, c, :].bitcast(F32), ALU.subtract).then_inc(y_lo_ready, 1)

                scans(0)
                gated_outputs(0, 4)
                scans(1)
                y_lo_part(0, 2)
                gated_outputs(4, 8)
                y_lo_part(2, 8)

            dve.memset(eps[:, :], EPS).then_inc(consts_set, 1)
            for _ in range(GATE_BANKS):
                dve.sem_inc(gated, 1)
            dve.wait_ge(consts_set, 3)
            norm(0)
            attention()
            peer(0)
            recurrent()
            peer(1)
            add = add_experts(1)
            for b in range(TB):
                add(b)

        @block.tensor
        def _(pe):
            def norm(n):
                for b in range(TB):
                    pe.wait_ge(diag_ready, TB * n + b + 1)
                    for m in range(KC // 2):
                        for c in (m, m + 4):
                            a = (c // 4) * SEQ + b * P
                            ins = pe.matmul(ps[NORM_BANK[n] + m][:, a:a + P], x[:, b, c * P:(c + 1) * P], x_diag[:, b, :],
                                            start=True, stop=True)
                        if b == TB - 1:
                            ins.then_inc(turned, 1)

            def hi_is_ready(n):
                pe.wait_ge(hi_ready, n + 1)

            def lo_is_ready(n):
                pe.wait_ge(lo_ready, n + 1 + RAW_SLOTS)

            def up_hi(k, c, o, start, pair=False):
                hi = t_hi[:, k, c * P:(c + 1) * P]
                pe.matmul(o, hi, h_hi[:, c, :], start=start, stop=False, skip_group_check=pair)
                pe.matmul(o, hi, h_lo[:, c, :], start=False, stop=False, skip_group_check=pair)

            def up_lo(n, k, o, pair=False):
                lo_is_ready(n)
                for c in range(KC):
                    ins = pe.matmul(o, t_lo[:, k % LO_SLOTS, c * P:(c + 1) * P], h_hi[:, c, :], start=False, stop=(c == KC - 1),
                                    skip_group_check=pair)
                ins.then_inc(tile_used, 1)

            def up_tile(n, k, o):
                hi_is_ready(n)
                for c in range(KC):
                    up_hi(k, c, o, c == 0)
                up_lo(n, k, o)

            def first_pair(n, o, norm):
                slots = [(n + j) % HI_SLOTS for j in range(2)]
                outs = [o[:, j * SEQ:(j + 1) * SEQ] for j in range(2)]
                for j in range(2):
                    hi_is_ready(n + j)
                for c in range(KC):
                    pe.wait_ge(h_hi_ready, KC * norm + c + 1)
                    pe.wait_ge(h_lo_ready, KC * norm + c + 1)
                    for j in range(2):
                        up_hi(slots[j], c, outs[j], c == 0 and j == 0, True)
                for j in range(2):
                    up_lo(n + j, slots[j], outs[j], True)

            def down_part(b, a, tile, bank, first=False, last=False):
                for n in range(2):
                    ins = pe.matmul(ps[bank + 2 * b + n][:, :], a[:, b * P:(b + 1) * P], tile[:, n * BANK:(n + 1) * BANK],
                                    start=first, stop=last, skip_group_check=True)
                return ins

            def down_tile(n, k, a_hi, a_lo, bank, first=False, last=False):
                hi_is_ready(n)
                for b in range(TB):
                    down_part(b, a_hi, t_hi[:, k, :], bank, first)
                    down_part(b, a_lo, t_hi[:, k, :], bank)
                lo_is_ready(n)
                for b in range(TB):
                    ins = down_part(b, a_hi, t_lo[:, k % LO_SLOTS, :], bank, False, last)
                ins.then_inc(tile_used, 1)

            def last_tiles(n0, a_hi, a_lo, bank):
                for b in range(TB):
                    for j in range(LO_SLOTS):
                        n = n0 + j
                        if b == 0:
                            hi_is_ready(n)
                        down_part(b, a_hi(j), t_hi[:, n % HI_SLOTS, :], bank)
                        down_part(b, a_lo(j), t_hi[:, n % HI_SLOTS, :], bank)
                        if b == 0:
                            lo_is_ready(n)
                        ins = down_part(b, a_hi(j), t_lo[:, n % LO_SLOTS, :], bank, False, j == LO_SLOTS - 1)
                        if b == TB - 1:
                            ins.then_inc(tile_used, 1)
                    if b == 0:
                        ins.then_inc(block0_summed, 1)

            def project(m, c):
                n = AT_QKV + m * KC + c
                if m == 0:
                    pe.wait_ge(h_hi_ready, c + 1)
                    pe.wait_ge(h_lo_ready, c + 1)
                down_tile(n, n % HI_SLOTS, h_hi[:, c, :], h_lo[:, c, :], 4 * ((m + 1) % 2), c == 0, c == KC - 1)

            def attention():
                for c in range(KC):
                    project(0, c)
                for c in range(KC):
                    project(1, c)
                pe.wait_ge(qkv_copied, 4)

                def turn_qk(b):
                    for k in range(2):
                        pe.wait_ge(qn_ready, TB * k + b + 1)
                        for m in range(2):
                            i = b * 4 + k * 2 + m
                            if i >= 4:
                                pe.wait_ge((q_turned, k_turned)[k], m + 1)
                            for c in range(4):
                                a = k * D + (4 * m + c) * P
                                ins = pe.transpose(ps[i % 4][:, c * P:(c + 1) * P], qkv[:, b, a:a + P], ident[:, :])
                            ins.then_inc(qk_psum, 1)

                def scores(s):
                    g, b = s // TB, s % TB
                    w = (b + 1) * P
                    if s >= 2:
                        pe.wait_ge(sc_ready, 2 * (s - 1))
                    for m in range(2):
                        for r in range(2):
                            rows = slice(r * HD, (r + 1) * HD)
                            ins = pe.matmul(ps[2 * (s % 2) + r][:, m * 2 * P:m * 2 * P + w], QT[rows, 2 * g + m, b * P:(b + 1) * P],
                                            KT[rows, 2 * g + m, 0:w], start=True, stop=True)
                    ins.then_inc(sc_psum, 1)

                def pt_banks(s):
                    return sum(1 + i % TB for i in range(s))

                def turn_probs(s):
                    b = s % TB
                    if s < TB:
                        pe.wait_ge(qkv_copied, 8 + b + 1)
                    pe.wait_ge(p_diag_ready, s + 1)
                    if s >= 1:
                        pe.wait_ge(pt_ready, pt_banks(s))
                    for h in range(4):
                        for k in range(b + 1):
                            i = h * (b + 1) + k
                            ins = pe.matmul(ps[4 + i // 4][:, (i % 4) * P:(i % 4 + 1) * P], Pr[:, s % 2, h, k * P:(k + 1) * P],
                                            p_diag[:, s % 2, h, :], start=True, stop=True)
                    ins.then_inc(pt_psum, 1)

                def weigh(s):
                    g, b = s // TB, s % TB
                    if s < TB:
                        pe.wait_ge(v1_copied, 2)
                    pe.wait_ge(pt_ready, pt_banks(s + 1))
                    if s >= 2:
                        pe.wait_ge(o_lo_ready, 2 * (s - 1))
                    for h in range(4):
                        for k in range(b + 1):
                            a = 2 * D + (4 * g + h // 2 * 2) * HD
                            ins = pe.matmul(ps[6 + s % 2][:, h * P:(h + 1) * P], qkv[:, k, a:a + 2 * HD], PT[:, s % 2, h * (b + 1) + k, :],
                                            start=(k == 0), stop=(k == b))
                    ins.then_inc(pv_psum, 1)

                def project_out(c):
                    outputs_ready(c)
                    down_tile(AT_WOUT + c, (AT_WOUT + c) % HI_SLOTS, h_hi[:, c, :], h_lo[:, c, :], OUT_BANK, c == 0)

                def outputs_ready(c):
                    pe.wait_ge(o_hi_ready, 4 * (c // 2 + 1))
                    pe.wait_ge(o_lo_ready, 4 * (c // 2 + 1))

                for c in range(4):
                    project(2, c)
                pe.wait_ge(qkv_copied, 8)
                turn_qk(0)
                project(2, 4)
                turn_qk(1)
                project(2, 5)
                pe.wait_ge(q_turned, 4)
                pe.wait_ge(k_turned, 4)
                scores(0)
                project(2, 6)
                scores(1)
                project(2, 7)
                for s in range(8):
                    if s < 6:
                        scores(s + 2)
                    turn_probs(s)
                    if s >= 1:
                        weigh(s - 1)
                project_out(0)
                weigh(7)
                for c in range(1, PROJ_TILES - LO_SLOTS):
                    project_out(c)
                outputs_ready(KC - 1)
                last_tiles(AT_WOUT + KC - LO_SLOTS, lambda j: h_hi[:, KC - LO_SLOTS + j, :], lambda j: h_lo[:, KC - LO_SLOTS + j, :],
                           OUT_BANK)

            def peer(l):
                n = 2 * l + 1
                norm(n)

                def key_scores(h):
                    pe.wait_ge(q_copied, l * PHEADS + h + 1)
                    if h >= 2:
                        pe.wait_ge(s_copied, l * PHEADS + h - 1)
                    for b in range(TB):
                        for k in range(2):
                            a = (2 * b + k) * NKEYS
                            ins = pe.matmul(ps[Q_BANK + 2 + h % 2][:, a:a + NKEYS], qT[:, h % 2, k, b * P:(b + 1) * P], keys[:, k, :],
                                            start=True, stop=True)
                    ins.then_inc(s_psum, 1)

                pe.wait_ge(keys_loaded, 16 * (l + 1))
                for h in range(PHEADS):
                    if h >= 2:
                        pe.wait_ge(q_copied, l * PHEADS + h - 1)
                    if h == 0:
                        first_pair(AT_WQ[l], ps[Q_BANK], n)
                    else:
                        for k in range(2):
                            i = AT_WQ[l] + 2 * h + k
                            up_tile(i, i % HI_SLOTS, ps[Q_BANK + h % 2][:, k * SEQ:(k + 1) * SEQ])
                    if h >= 1:
                        key_scores(h - 1)
                key_scores(PHEADS - 1)

                def up(g, k, half):
                    if k % 2 == 0:
                        pe.wait_ge(act_ready, g * 2 + (l * TILES // 2 + half * HALF // 2 + k // 2 + 1))
                    up_tile(g * UNROLL + (AT_U[l] + half * HALF + k), k, ps[UP_BANK + k // 2][:, (k % 2) * SEQ:(k % 2 + 1) * SEQ])

                def gates(g, k, half):
                    n = g * UNROLL + ((l * 2 + half) * GROUPS + k + 1)
                    pe.wait_ge(hot_ready, n)
                    pe.wait_ge(gated, n)
                    for t in range(GROUP):
                        for part in range(PARTS):
                            ins = pe.matmul(ps[2 + k % 2][:, t * HALF:(t + 1) * HALF], hot1[:, k % 2, t, :], hot2[:, k % 2, t, part, :],
                                            start=(part == 0), stop=(part == PARTS - 1))
                    ins.then_inc(gates_psum, 1)

                with pe.Fori(0, TURN_AT) as g:
                    for k in range(UNROLL):
                        up(g, k, 0)
                pe.wait_ge(slots_ready, l + 1)
                for w in range(3):
                    for b in range(TB):
                        a = (w % 2) * SEQ + b * P
                        ins = pe.transpose(ps[2 + w // 2][:, a:a + P], slot[:, w, b, :], ident[:, :])
                ins.then_inc(slot_psum, 1)
                with pe.Fori(TURN_AT, BODIES) as g:
                    for k in range(UNROLL):
                        up(g, k, 0)
                with pe.Fori(0, BODIES) as g:
                    for k in range(UNROLL):
                        if k % 2 == 0:
                            gates(g, k, 0)
                            gates(g, k + 1, 0)
                        up(g, k, 1)

                def down(g, k, half, first=False):
                    pe.wait_ge(wlo_ready, g * UNROLL + (l * TILES + half * HALF + k + 1))
                    down_tile(g * UNROLL + (AT_U[l] + TILES + half * HALF + k), k, w_hi[:, k, :], w_lo[:, k, :], 4, first)

                for k in range(UNROLL):
                    gates(0, k, 1)
                    if k == 0:
                        pe.wait_ge(act_ready, (l + 1) * TILES // 2 + 2)
                    down(0, k, 0, k == 0)
                with pe.Fori(1, BODIES) as g:
                    for k in range(UNROLL):
                        if k % 2 == 0:
                            gates(g, k, 1)
                            gates(g, k + 1, 1)
                        down(g, k, 0)
                with pe.Fori(0, BODIES - 1) as g:
                    for k in range(UNROLL):
                        down(g, k, 1)
                for k in range(UNROLL - LO_SLOTS):
                    down(BODIES - 1, k, 1)
                pe.wait_ge(wlo_ready, (l + 1) * TILES)
                last_tiles(AT_U[l] + 2 * TILES - LO_SLOTS, lambda j: w_hi[:, UNROLL - LO_SLOTS + j, :],
                           lambda j: w_lo[:, UNROLL - LO_SLOTS + j, :], 4)

            def recurrent():
                norm(2)
                pe.wait_ge(x_stored, 4)

                def channels(i):
                    if i >= 4:
                        pe.wait_ge(rec_copied, i - 3)
                    for j in range(2):
                        n = AT_WIN + 2 * i + j
                        up_tile(n, n % HI_SLOTS, ps[4 + i % 4][:, j * SEQ:(j + 1) * SEQ])

                def lru_gates(h):
                    pe.wait_ge(conv_done, 2 * (h + 1))
                    for g in range(2):
                        i = 2 * h + g
                        if i >= 4:
                            pe.wait_ge(rg_ready, 2 * (i - 3))
                        for j in range(2):
                            for c in range(2):
                                ins = pe.matmul(ps[i % 4][:, j * SEQ:(j + 1) * SEQ], wax[:, g, h, c, j * P:(j + 1) * P], uc[:, 2 * h + c, :],
                                                start=(c == 0), stop=(c == 1))
                        ins.then_inc(rg_psum, 1)

                first_pair(AT_WIN, ps[4], 2)
                for i in range(1, 3):
                    channels(i)
                pe.wait_ge(wax_loaded, 16)
                lru_gates(0)
                channels(3)
                for h in range(1, LRU_HEADS):
                    lru_gates(h)
                for i in range(4, 8):
                    channels(i)
                for c in range(KC - LO_SLOTS):
                    pe.wait_ge(y_hi_ready, c + 1)
                    pe.wait_ge(y_lo_ready, c + 1)
                    down_tile(AT_RWOUT + c, (AT_RWOUT + c) % HI_SLOTS, h_hi[:, c, :], h_lo[:, c, :], OUT_BANK, c == 0)
                pe.wait_ge(y_hi_ready, KC)
                pe.wait_ge(y_lo_ready, KC)
                last_tiles(AT_RWOUT + KC - LO_SLOTS, lambda j: h_hi[:, KC - LO_SLOTS + j, :], lambda j: h_lo[:, KC - LO_SLOTS + j, :],
                           OUT_BANK)

            for _ in range(HI_SLOTS):
                pe.sem_inc(tile_used, 1)
            for _ in range(GATE_BANKS):
                pe.sem_inc(gates_psum, 1)
            pe.wait_ge(consts_set, 3)
            norm(0)
            attention()
            peer(0)
            recurrent()
            peer(1)


def kernel(**inputs):
    import numpy as np
    import concourse.bacc as bacc
    from concourse.bass_utils import run_bass_kernel_spmd

    a = {k: np.asarray(v) for k, v in inputs.items()}

    def by_chunk(v):
        return v.reshape(KC, P).T

    windows = np.lib.stride_tricks.sliding_window_view(a["attn_rel_bias"][0][:, ::-1], 2 * P, axis=1)
    def up_tiles(w):
        return w.reshape(KC, P, -1, P).transpose(2, 1, 0, 3).reshape(-1, P, D)

    win = up_tiles(a["rec_w_in"][0])
    u = a["peer_u"].reshape(2, NKEYS, NKEYS, KC, P)
    arrays = {
        "x_in": a["x"].reshape(SEQ, D),
        "norm_g": np.stack([by_chunk(v) for v in (a["attn_norm_g"][0], a["ffn_norm_g"][0], a["rec_norm_g"][0],
                                                  a["ffn_norm_g"][1])], axis=1),
        "w_qkv": a["attn_w_qkv"][0],
        "qk_g": np.stack([np.concatenate([v, v]) for v in (a["attn_q_g"][0], a["attn_k_g"][0])], axis=1),
        "rel_rows": windows[:, P:0:-1].transpose(1, 0, 2),
        "w_out": a["attn_w_out"][0],
        "w_in": np.concatenate([win[KC:], win[:KC]]),
        "rec_p": np.stack([by_chunk(v) for v in (*a["rec_conv_w"][0], a["rec_conv_b"][0], a["rec_b_a"][0],
                                                 a["rec_b_x"][0], a["rec_lambda"][0])], axis=2),
        "w_ax": np.stack([a[n][0].reshape(LRU_HEADS, 2, P, 2 * P).transpose(2, 0, 1, 3) for n in ("rec_w_a", "rec_w_x")], axis=1),
        "rec_w_out": a["rec_w_out"][0],
        "w_q": np.stack([up_tiles(w) for w in a["peer_w_q"]]),
        "keys_t": a["peer_sub_keys"].transpose(0, 3, 1, 2),
        "u_t": u.transpose(0, 2, 4, 3, 1).reshape(2, TILES, P, D),
        "v_t": a["peer_v"].reshape(2, NKEYS, NKEYS, D),
    }
    arrays = {k: np.ascontiguousarray(v) for k, v in arrays.items()}
    nc = bacc.Bacc("TRN2", target_bir_lowering=False, num_devices=1)
    args = {k: nc.dram_tensor(k, v.shape, F32, kind="ExternalInput").ap() for k, v in arrays.items()}
    args["v_t"] = args["v_t"].rearrange("l i j d -> l j i d")
    args["out"] = nc.dram_tensor("out", (SEQ, D), F32, kind="ExternalOutput").ap()
    trunk(nc, **args)
    r = run_bass_kernel_spmd(nc, [arrays], core_ids=[0])
    return r.results[0]["out"].reshape(1, SEQ, D)
```
